# Optimizing a Trainium2 kernel written in Bass

```python
import math
import jax, jax.numpy as jnp
from jax import lax
import numpy as np
import jax
import jax.numpy as jnp

D_MODEL = 2048
BATCH = 1
SEQ = 256
DEPTH = 1

N_MEM = 256
D_MIX = 2 * D_MODEL
D_SSD = D_MIX // 2
D_SC = D_MIX - D_SSD
SSD_HEADDIM = 64
SSD_HEADS = D_SSD // SSD_HEADDIM
SSD_GROUPS = 4
SSD_STATE = 128
SSD_CONV = 4
SSD_CHUNK = 256
D_XBC = D_SSD + 2 * SSD_GROUPS * SSD_STATE
DT_MIN = 1e-3
DT_MAX = 1e-1
SC_CONV = 3
SC_GROUPS = 16
XA_HEADS = 4
XA_HEADDIM = 128
D_XA = XA_HEADS * XA_HEADDIM
D_FF = ((8 * D_MODEL + 3 * 256 - 1) // (3 * 256)) * 256
NORM_EPS = 1e-5
D_IN_PROJ = D_SSD + D_XBC + SSD_HEADS + 3 * D_SC
IN_SPLITS = [D_SSD,
             D_SSD + D_XBC,
             D_SSD + D_XBC + SSD_HEADS,
             D_SSD + D_XBC + SSD_HEADS + D_SC,
             D_SSD + D_XBC + SSD_HEADS + 2 * D_SC]


def rmsnorm(x, g):
    xf = x.astype(jnp.float32)
    xf = xf * lax.rsqrt(jnp.mean(xf * xf, axis=-1, keepdims=True) + NORM_EPS)
    return (xf * g.astype(jnp.float32)).astype(x.dtype)

def grouped_rmsnorm(x, g, n_groups):
    shp = x.shape
    xf = x.astype(jnp.float32).reshape(shp[:-1] + (n_groups, shp[-1] // n_groups))
    xf = xf * lax.rsqrt(jnp.mean(xf * xf, axis=-1, keepdims=True) + NORM_EPS)
    return (xf.reshape(shp) * g.astype(jnp.float32)).astype(x.dtype)

def causal_dwconv(x, w):
    k, c = w.shape
    return lax.conv_general_dilated(
        x, w[:, None, :].astype(x.dtype), window_strides=(1,), padding=[(k - 1, 0)],
        dimension_numbers=("NWC", "WIO", "NWC"), feature_group_count=c)

def ssd_chunked(xh, dt, a, bm, cm):
    f32 = jnp.float32
    bsz, seqlen, nh, hd = xh.shape
    g, n = bm.shape[2], bm.shape[3]
    r = nh // g
    pad = (-seqlen) % SSD_CHUNK
    xh, dt, bm, cm = (t.astype(f32) for t in (xh, dt, bm, cm))
    if pad:
        xh = jnp.pad(xh, ((0, 0), (0, pad), (0, 0), (0, 0)))
        dt = jnp.pad(dt, ((0, 0), (0, pad), (0, 0)))
        bm = jnp.pad(bm, ((0, 0), (0, pad), (0, 0), (0, 0)))
        cm = jnp.pad(cm, ((0, 0), (0, pad), (0, 0), (0, 0)))
    nc = (seqlen + pad) // SSD_CHUNK
    L = SSD_CHUNK
    x = (xh * dt[..., None]).reshape(bsz, nc, L, g, r, hd)
    a_dt = jnp.moveaxis((dt * a.astype(f32)).reshape(bsz, nc, L, g, r), 2, -1)
    a_cs = jnp.cumsum(a_dt, axis=-1)
    bc = bm.reshape(bsz, nc, L, g, n)
    cc = cm.reshape(bsz, nc, L, g, n)
    causal = jnp.tril(jnp.ones((L, L), dtype=bool))
    decay = jnp.exp(jnp.where(causal, a_cs[..., :, None] - a_cs[..., None, :], -jnp.inf))
    cb = jnp.einsum("bclgn,bcsgn->bcgls", cc, bc)
    scores = cb[:, :, :, None] * decay
    y_diag = jnp.einsum("bcgrls,bcsgrp->bclgrp", scores, x)
    decay_states = jnp.exp(a_cs[..., -1:] - a_cs)
    states = jnp.einsum("bclgn,bcgrl,bclgrp->bcgrpn", bc, decay_states, x)
    chunk_decay = jnp.exp(a_cs[..., -1])

    def step(h, inp):
        s_c, d_c = inp
        return h * d_c[..., None, None] + s_c, h

    h0 = jnp.zeros_like(states[:, 0])
    _, prev = lax.scan(step, h0, (jnp.moveaxis(states, 1, 0), jnp.moveaxis(chunk_decay, 1, 0)))
    prev = jnp.moveaxis(prev, 0, 1)
    y_off = jnp.einsum("bclgn,bcgrpn,bcgrl->bclgrp", cc, prev, jnp.exp(a_cs))
    y = (y_diag + y_off).reshape(bsz, nc * L, nh, hd)
    return y[:, :seqlen]

def hybrid_mixer(h, w_in, ssd_conv_w, ssd_conv_b, dt_bias, a_log, d_skip, ssd_norm,
                 sc_conv_w, sc_norm, w_out):
    bsz, seqlen, _ = h.shape
    proj = h @ w_in
    z, xbc, dt_raw, sc_u, sc_b, sc_c = jnp.split(proj, IN_SPLITS, axis=-1)
    xbc = jax.nn.silu(causal_dwconv(xbc, ssd_conv_w) + ssd_conv_b)
    xs, bm, cm = jnp.split(xbc, [D_SSD, D_SSD + SSD_GROUPS * SSD_STATE], axis=-1)
    xh = xs.reshape(bsz, seqlen, SSD_HEADS, SSD_HEADDIM)
    dt = jax.nn.softplus(dt_raw.astype(jnp.float32) + dt_bias.astype(jnp.float32))
    a = -jnp.exp(a_log.astype(jnp.float32))
    y = ssd_chunked(xh, dt, a,
                    bm.reshape(bsz, seqlen, SSD_GROUPS, SSD_STATE),
                    cm.reshape(bsz, seqlen, SSD_GROUPS, SSD_STATE))
    y = y + xh.astype(jnp.float32) * d_skip.astype(jnp.float32)[:, None]
    y = y.reshape(bsz, seqlen, D_SSD).astype(h.dtype)
    y_ssd = grouped_rmsnorm(y * jax.nn.silu(z), ssd_norm, SSD_GROUPS)
    v = sc_b * causal_dwconv(sc_c * sc_u, sc_conv_w)
    y_sc = grouped_rmsnorm(v, sc_norm, SC_GROUPS)
    return jnp.concatenate([y_ssd, y_sc], axis=-1) @ w_out

def memory_cross_attention(h, mem_n, w_q, w_k, w_v, w_o):
    bsz, seqlen, _ = h.shape
    n_mem = mem_n.shape[1]
    q = (h @ w_q).reshape(bsz, seqlen, XA_HEADS, XA_HEADDIM)
    k = (mem_n @ w_k).reshape(bsz, n_mem, XA_HEADS, XA_HEADDIM)
    v = (mem_n @ w_v).reshape(bsz, n_mem, XA_HEADS, XA_HEADDIM)
    scores = jnp.einsum("bshd,bmhd->bhsm", q, k).astype(jnp.float32) * (XA_HEADDIM ** -0.5)
    p = jax.nn.softmax(scores, axis=-1).astype(v.dtype)
    o = jnp.einsum("bhsm,bmhd->bshd", p, v).reshape(bsz, seqlen, D_XA)
    return o @ w_o

def swiglu(h, w_gate, w_up, w_down):
    return (jax.nn.silu(h @ w_gate) * (h @ w_up)) @ w_down

def first_inputs(seed: int = 0) -> dict:
    key = jax.random.key(seed)
    ks = jax.random.split(key, 24)
    f32 = jnp.float32

    def nrm(k, shape, scale):
        return jax.random.normal(k, shape, f32) * scale

    def gain(k, shape):
        return 1.0 + 0.02 * jax.random.normal(k, shape, f32)

    x = nrm(ks[0], (BATCH, SEQ, D_MODEL), 1.0)
    mem = nrm(ks[1], (BATCH, N_MEM, D_MODEL), 1.0)
    norm_mix = gain(ks[2], (DEPTH, D_MODEL))
    w_in = nrm(ks[3], (DEPTH, D_MODEL, D_IN_PROJ), D_MODEL ** -0.5)
    ssd_conv_w = nrm(ks[4], (DEPTH, SSD_CONV, D_XBC), SSD_CONV ** -0.5)
    ssd_conv_b = nrm(ks[5], (DEPTH, D_XBC), 0.02)
    dt0 = jnp.exp(jax.random.uniform(ks[6], (DEPTH, SSD_HEADS), f32, math.log(DT_MIN), math.log(DT_MAX)))
    dt_bias = dt0 + jnp.log(-jnp.expm1(-dt0))
    a_log = jnp.log(jax.random.uniform(ks[7], (DEPTH, SSD_HEADS), f32, 1.0, 16.0))
    d_skip = gain(ks[8], (DEPTH, SSD_HEADS))
    ssd_norm = gain(ks[9], (DEPTH, D_SSD))
    sc_conv_w = nrm(ks[10], (DEPTH, SC_CONV, D_SC), SC_CONV ** -0.5)
    sc_norm = gain(ks[11], (DEPTH, D_SC))
    w_out = nrm(ks[12], (DEPTH, D_MIX, D_MODEL), D_MIX ** -0.5)
    mem_norm = gain(ks[13], (D_MODEL,))
    norm_xa = gain(ks[14], (DEPTH, D_MODEL))
    w_q = nrm(ks[15], (DEPTH, D_MODEL, D_XA), D_MODEL ** -0.5)
    w_k = nrm(ks[16], (DEPTH, D_MODEL, D_XA), D_MODEL ** -0.5)
    w_v = nrm(ks[17], (DEPTH, D_MODEL, D_XA), D_MODEL ** -0.5)
    w_o = nrm(ks[18], (DEPTH, D_XA, D_MODEL), D_XA ** -0.5)
    norm_ffn = gain(ks[19], (DEPTH, D_MODEL))
    w_gate = nrm(ks[20], (DEPTH, D_MODEL, D_FF), D_MODEL ** -0.5)
    w_up = nrm(ks[21], (DEPTH, D_MODEL, D_FF), D_MODEL ** -0.5)
    w_down = nrm(ks[22], (DEPTH, D_FF, D_MODEL), D_FF ** -0.5)
    norm_final = gain(ks[23], (D_MODEL,))
    return {"x": x, "mem": mem, "norm_mix": norm_mix, "w_in": w_in,
            "ssd_conv_w": ssd_conv_w, "ssd_conv_b": ssd_conv_b, "dt_bias": dt_bias,
            "a_log": a_log, "d_skip": d_skip, "ssd_norm": ssd_norm,
            "sc_conv_w": sc_conv_w, "sc_norm": sc_norm, "w_out": w_out,
            "mem_norm": mem_norm, "norm_xa": norm_xa, "w_q": w_q, "w_k": w_k,
            "w_v": w_v, "w_o": w_o, "norm_ffn": norm_ffn, "w_gate": w_gate,
            "w_up": w_up, "w_down": w_down, "norm_final": norm_final}

def first_block(x, mem, norm_mix, w_in, ssd_conv_w, ssd_conv_b, dt_bias, a_log, d_skip,
              ssd_norm, sc_conv_w, sc_norm, w_out, mem_norm, norm_xa, w_q, w_k, w_v, w_o,
              norm_ffn, w_gate, w_up, w_down, norm_final):
    mem_n = rmsnorm(mem, mem_norm)
    h = x
    for i in range(DEPTH):
        h = h + hybrid_mixer(rmsnorm(h, norm_mix[i]), w_in[i], ssd_conv_w[i], ssd_conv_b[i],
                             dt_bias[i], a_log[i], d_skip[i], ssd_norm[i],
                             sc_conv_w[i], sc_norm[i], w_out[i])
        h = h + memory_cross_attention(rmsnorm(h, norm_xa[i]), mem_n, w_q[i], w_k[i], w_v[i], w_o[i])
        h = h + swiglu(rmsnorm(h, norm_ffn[i]), w_gate[i], w_up[i], w_down[i])
    return rmsnorm(h, norm_final)


CHUNK = 64
Q_BLOCK = 128
HEAD_DIM = 64
N_HEADS_DIFF = D_MODEL // (4 * HEAD_DIM)
N_HEADS_SB = D_MODEL // (4 * HEAD_DIM)
N_HEADS_CH = D_MODEL // (4 * HEAD_DIM)
DIFF_WIDTH = N_HEADS_DIFF * 2 * HEAD_DIM
SB_WIDTH = N_HEADS_SB * HEAD_DIM
CH_WIDTH = N_HEADS_CH * HEAD_DIM
MIX_WIDTH = DIFF_WIDTH + SB_WIDTH + CH_WIDTH
QKV_WIDTH = 3 * MIX_WIDTH
LEFT_CHUNKS = 8
BAND = (LEFT_CHUNKS + 1) * CHUNK
MAX_REL = 128
N_REL = (CHUNK - 1) + MAX_REL + 1
D_FF_2 = 5632
CONV_WIDTH = 3
NORM_EPS_2 = 1e-6
SUBLN_EPS = 1e-5


def rmsnorm_2(x, g, eps=NORM_EPS_2):
    xf = x.astype(jnp.float32)
    y = xf * lax.rsqrt(jnp.mean(xf * xf, axis=-1, keepdims=True) + eps)
    return (y * g.astype(jnp.float32)).astype(x.dtype)

def alibi_slopes(n):
    return 2.0 ** (-8.0 * jnp.arange(1, n + 1, dtype=jnp.float32) / n)

def to_query_blocks(t):
    b, h, s = t.shape[:3]
    t = t.reshape((b, h, s // Q_BLOCK, Q_BLOCK) + t.shape[3:])
    return jnp.moveaxis(t, 2, 0)

def from_query_blocks(o):
    nb, b, h, qb, dv = o.shape
    return o.transpose(1, 0, 3, 2, 4).reshape(b, nb * qb, h * dv)

def split_columns(qkv):
    widths = [DIFF_WIDTH] * 3 + [SB_WIDTH] * 3 + [CH_WIDTH] * 3
    outs, start = [], 0
    for w in widths:
        outs.append(qkv[..., start:start + w])
        start += w
    return outs

def diff_attention(q, k, v, lam, lam_init, subln_g):
    b, s, _ = q.shape
    h = N_HEADS_DIFF
    q = q.reshape(b, s, h, 2, HEAD_DIM).transpose(0, 2, 1, 3, 4)
    k = k.reshape(b, s, h, 2, HEAD_DIM).transpose(0, 2, 1, 3, 4)
    v = v.reshape(b, s, h, 2 * HEAD_DIM).transpose(0, 2, 1, 3)
    slopes = alibi_slopes(h)
    k_pos = jnp.arange(s)
    k_chunk = k_pos // CHUNK
    scale = HEAD_DIM ** -0.5

    def block(args):
        q_blk, i = args
        q_pos = i * Q_BLOCK + jnp.arange(Q_BLOCK)
        sc = jnp.einsum('bhqcd,bhkcd->bhcqk', q_blk, k).astype(jnp.float32) * scale
        dist = jnp.abs(q_pos[:, None] - k_pos[None, :]).astype(jnp.float32)
        bias = -slopes[:, None, None] * dist
        allowed = k_chunk[None, :] <= (q_pos // CHUNK)[:, None]
        sc = jnp.where(allowed, sc + bias[None, :, None], -jnp.inf)
        p = jax.nn.softmax(sc, axis=-1)
        w = (p[:, :, 0] - lam * p[:, :, 1]).astype(v.dtype)
        return jnp.einsum('bhqk,bhkv->bhqv', w, v)

    o = lax.map(block, (to_query_blocks(q), jnp.arange(s // Q_BLOCK)))
    o = rmsnorm_2(o, subln_g, SUBLN_EPS) * (1.0 - lam_init)
    return from_query_blocks(o)

def stick_breaking_attention(q, k, v, head_g):
    b, s, _ = q.shape
    h = N_HEADS_SB
    q = q.reshape(b, s, h, HEAD_DIM).transpose(0, 2, 1, 3)
    k = k.reshape(b, s, h, HEAD_DIM).transpose(0, 2, 1, 3)
    v = v.reshape(b, s, h, HEAD_DIM).transpose(0, 2, 1, 3)
    k_pos = jnp.arange(s)
    scale = HEAD_DIM ** -0.5

    def block(args):
        q_blk, i = args
        q_pos = i * Q_BLOCK + jnp.arange(Q_BLOCK)
        z = jnp.einsum('bhqd,bhkd->bhqk', q_blk, k).astype(jnp.float32) * scale
        causal = k_pos[None, :] < q_pos[:, None]
        log_1m_beta = jnp.where(causal, -jax.nn.softplus(z), 0.0)
        suffix = lax.cumsum(log_1m_beta, axis=3, reverse=True) - log_1m_beta
        log_a = jax.nn.log_sigmoid(z) + suffix
        a = jnp.where(causal, jnp.exp(log_a), 0.0).astype(v.dtype)
        return jnp.einsum('bhqk,bhkd->bhqd', a, v)

    o = lax.map(block, (to_query_blocks(q), jnp.arange(s // Q_BLOCK)))
    o = rmsnorm_2(o, head_g[:, None, :])
    return from_query_blocks(o)

def chunk_band_attention(q, k, v, rel_table, head_g):
    b, s, _ = q.shape
    h = N_HEADS_CH
    nc = s // CHUNK
    pad = LEFT_CHUNKS * CHUNK
    q = q.reshape(b, s, h, HEAD_DIM).transpose(0, 2, 1, 3)
    k = k.reshape(b, s, h, HEAD_DIM).transpose(0, 2, 1, 3)
    v = v.reshape(b, s, h, HEAD_DIM).transpose(0, 2, 1, 3)
    qc = q.reshape(b, h, nc, CHUNK, HEAD_DIM)

    def band(t):
        tp = jnp.pad(t, ((0, 0), (0, 0), (pad, 0), (0, 0)))
        tp = tp.reshape(b, h, nc + LEFT_CHUNKS, CHUNK, HEAD_DIM)
        return jnp.concatenate([tp[:, :, o:o + nc] for o in range(LEFT_CHUNKS + 1)], axis=3)

    kb, vb = band(k), band(v)
    sc = jnp.einsum('bhcqd,bhckd->bhcqk', qc, kb).astype(jnp.float32) * HEAD_DIM ** -0.5
    q_loc = jnp.arange(CHUNK)
    k_loc = jnp.arange(BAND) - pad
    rel_idx = jnp.clip(q_loc[:, None] - k_loc[None, :], -(CHUNK - 1), MAX_REL) + (CHUNK - 1)
    bias = rel_table[:, rel_idx].astype(jnp.float32)
    valid = (jnp.arange(nc)[:, None] * CHUNK + k_loc[None, :]) >= 0
    sc = jnp.where(valid[:, None, :], sc + bias[:, None], -jnp.inf)
    p = jax.nn.softmax(sc, axis=-1).astype(vb.dtype)
    o = jnp.einsum('bhcqk,bhckd->bhcqd', p, vb).reshape(b, h, s, HEAD_DIM)
    o = rmsnorm_2(o, head_g[:, None, :])
    return o.transpose(0, 2, 1, 3).reshape(b, s, h * HEAD_DIM)

def causal_dwconv_2(hid, w, bias):
    s = hid.shape[1]
    hp = jnp.pad(hid, ((0, 0), (CONV_WIDTH - 1, 0), (0, 0)))
    out = bias
    for j in range(CONV_WIDTH):
        out = out + hp[:, j:j + s] * w[j]
    return out

def second_inputs(seed: int = 0) -> dict:
    key = jax.random.key(seed)
    ks = jax.random.split(key, 20)

    def nrm(k, shape, scale):
        return jax.random.normal(k, shape, jnp.float32) * scale

    def gain(k, shape):
        return 1.0 + nrm(k, shape, 0.05)

    return {
        'x': nrm(ks[0], (BATCH, SEQ, D_MODEL), 1.0),
        'attn_norm': gain(ks[1], (DEPTH, D_MODEL)),
        'w_qkv': nrm(ks[2], (DEPTH, D_MODEL, QKV_WIDTH), D_MODEL ** -0.5),
        'lambda_q1': nrm(ks[3], (DEPTH, HEAD_DIM), 0.1),
        'lambda_k1': nrm(ks[4], (DEPTH, HEAD_DIM), 0.1),
        'lambda_q2': nrm(ks[5], (DEPTH, HEAD_DIM), 0.1),
        'lambda_k2': nrm(ks[6], (DEPTH, HEAD_DIM), 0.1),
        'diff_subln': gain(ks[7], (DEPTH, 2 * HEAD_DIM)),
        'sb_norm': gain(ks[8], (DEPTH, N_HEADS_SB, HEAD_DIM)),
        'rel_bias': nrm(ks[9], (DEPTH, N_HEADS_CH, N_REL), 0.2),
        'ch_norm': gain(ks[10], (DEPTH, N_HEADS_CH, HEAD_DIM)),
        'w_o': nrm(ks[11], (DEPTH, MIX_WIDTH, D_MODEL), MIX_WIDTH ** -0.5),
        'ffn_norm': gain(ks[12], (DEPTH, D_MODEL)),
        'w_gate': nrm(ks[13], (DEPTH, D_MODEL, D_FF_2), D_MODEL ** -0.5),
        'w_up': nrm(ks[14], (DEPTH, D_MODEL, D_FF_2), D_MODEL ** -0.5),
        'conv_w': nrm(ks[15], (DEPTH, CONV_WIDTH, D_FF_2), CONV_WIDTH ** -0.5),
        'conv_b': nrm(ks[16], (DEPTH, D_FF_2), 0.02),
        'w_down': nrm(ks[17], (DEPTH, D_FF_2, D_MODEL), D_FF_2 ** -0.5),
        'final_norm': gain(ks[18], (D_MODEL,)),
    }

def second_block(x, attn_norm, w_qkv, lambda_q1, lambda_k1, lambda_q2, lambda_k2,
              diff_subln, sb_norm, rel_bias, ch_norm, w_o, ffn_norm, w_gate, w_up,
              conv_w, conv_b, w_down, final_norm):
    for l in range(DEPTH):
        lam_init = 0.8 - 0.6 * math.exp(-0.3 * l)
        h = rmsnorm_2(x, attn_norm[l])
        qkv = jnp.einsum('bsd,de->bse', h, w_qkv[l])
        q_a, k_a, v_a, q_b, k_b, v_b, q_c, k_c, v_c = split_columns(qkv)
        lam = (jnp.exp(jnp.sum(lambda_q1[l] * lambda_k1[l]).astype(jnp.float32))
               - jnp.exp(jnp.sum(lambda_q2[l] * lambda_k2[l]).astype(jnp.float32))
               + lam_init)
        y_a = diff_attention(q_a, k_a, v_a, lam, lam_init, diff_subln[l])
        y_b = stick_breaking_attention(q_b, k_b, v_b, sb_norm[l])
        y_c = chunk_band_attention(q_c, k_c, v_c, rel_bias[l], ch_norm[l])
        y = jnp.concatenate([y_a, y_b, y_c], axis=-1)
        x = x + jnp.einsum('bse,ed->bsd', y, w_o[l])
        h = rmsnorm_2(x, ffn_norm[l])
        g = causal_dwconv_2(jnp.einsum('bsd,df->bsf', h, w_gate[l]), conv_w[l], conv_b[l])
        u = jnp.einsum('bsd,df->bsf', h, w_up[l])
        x = x + jnp.einsum('bsf,fd->bsd', jax.nn.silu(g) * u, w_down[l])
    return rmsnorm_2(x, final_norm)


def setup_inputs(seed=0):
    out = dict(first_inputs(seed))
    for name, value in second_inputs(seed + 1).items():
        if name != "x":
            out[name + "_2"] = value
    return out


def reference(
    x, mem, norm_mix, w_in, ssd_conv_w, ssd_conv_b, dt_bias, a_log, d_skip, ssd_norm, sc_conv_w,
    sc_norm, w_out, mem_norm, norm_xa, w_q, w_k, w_v, w_o, norm_ffn, w_gate, w_up, w_down,
    norm_final, attn_norm_2, w_qkv_2, lambda_q1_2, lambda_k1_2, lambda_q2_2, lambda_k2_2,
    diff_subln_2, sb_norm_2, rel_bias_2, ch_norm_2, w_o_2, ffn_norm_2, w_gate_2, w_up_2,
    conv_w_2, conv_b_2, w_down_2, final_norm_2,
):
    x = first_block(
        x, mem, norm_mix, w_in, ssd_conv_w, ssd_conv_b, dt_bias, a_log, d_skip, ssd_norm,
        sc_conv_w, sc_norm, w_out, mem_norm, norm_xa, w_q, w_k, w_v, w_o, norm_ffn, w_gate,
        w_up, w_down, norm_final,
    )
    return second_block(
        x, attn_norm_2, w_qkv_2, lambda_q1_2, lambda_k1_2, lambda_q2_2, lambda_k2_2,
        diff_subln_2, sb_norm_2, rel_bias_2, ch_norm_2, w_o_2, ffn_norm_2, w_gate_2, w_up_2,
        conv_w_2, conv_b_2, w_down_2, final_norm_2,
    )


_drawn_inputs = setup_inputs


def setup_inputs(seed=0):
    import zlib

    import numpy as np

    out = dict(_drawn_inputs(seed))
    spreads = {}
    factors = {'d_skip': 6.176,
     'ssd_norm': 3.839,
     'sc_norm': 4.28,
     'mem_norm': 8.0,
     'norm_xa': 8.0,
     'norm_ffn': 4.111,
     'lambda_q2_2': 8.0,
     'lambda_k2_2': 7.822,
     'diff_subln_2': 2.747,
     'sb_norm_2': 2.841,
     'ch_norm_2': 2.889,
     'conv_b_2': 7.018,
     'lambda_q1_2': 64.0,
     'lambda_k1_2': 8.0,
     'ffn_norm_2': 3.43}
    for name, (base, spread) in spreads.items():
        noise = np.random.default_rng([zlib.crc32(name.encode()), seed]).standard_normal(out[name].shape)
        drawn = base * np.exp(spread * noise) if base else spread * noise
        out[name] = jnp.asarray(drawn.astype(out[name].dtype))
    for name, factor in factors.items():
        out[name] = (out[name] * factor).astype(out[name].dtype)
    return out
```

```python
from contextlib import ExitStack

import numpy as np

import concourse.bass as bass
from concourse import mybir

F32 = mybir.dt.float32
F32R = mybir.dt.float32r
ALU = mybir.AluOpType
ACT = mybir.ActivationFunctionType
AX = mybir.AxisListType.X

P = 128
T = 256
BLK = 128
SUB = 8 * BLK
UNIT = 2 * SUB
NRAW = 3
NW = 4
NEG = -1e30

PARTS = [(0, 16), (16, 32), (32, 44)]

VEC = [
    ("norm_mix", 16), ("ssd_conv_w", 96), ("ssd_conv_b", 24), ("sc_conv_w", 48), ("sc_norm", 16),
    ("ssd_norm", 16), ("norm_xa", 16), ("mem_norm", 16), ("norm_ffn", 16), ("norm_final", 16),
    ("attn_norm_2", 16), ("diff_subln_2", 1), ("sb_norm_2", 4), ("ch_norm_2", 4), ("ffn_norm_2", 16),
    ("conv_w_2", 132), ("conv_b_2", 44), ("final_norm_2", 16), ("dt_bias", 1), ("a_log", 32),
    ("d_skip", 32), ("eps5", 1), ("eps6", 1),
]
VOFF = {}
_o = 0
for _n, _w in VEC:
    VOFF[_n] = (_o, _w)
    _o += _w
NVEC = _o

C1 = [("ident", 128), ("tri", 384), ("mneg", 128)]
C2 = [("bd", 128), ("tri2", 128), ("flip", 128), ("nm", 384), ("cm", 384), ("dist", 384), ("mc", 64), ("lam", 256)]


def offsets(table):
    out, at = {}, 0
    for name, w in table:
        out[name] = (at, w)
        at += w
    return out, at


C1OFF, NC1 = offsets(C1)
C2OFF, NC2 = offsets(C2)

UNITS = [("w_in", 89), ("w_out", 32), ("w_k", 4), ("w_v", 4), ("w_q", 4), ("w_o", 4), ("ffn", 132),
         ("w_qkv_2", 48), ("w_o_2", 16), ("ffn_2", 132)]


class Engine:

    def __init__(self, sem):
        self.sem, self.n, self.todo = sem, 0, []

    def __call__(self, fn, *waits, sig=True):
        if sig:
            self.n += 1
        self.todo.append((waits, fn, self.sem if sig else None))
        return (self.sem, self.n)

    def dma(self, out, in_, sem, *waits):
        self.todo.append((waits, lambda e: e.dma_start(out, in_).then_inc(sem, 16), None))

    def play(self, e):
        seen = {}
        for waits, fn, sem in self.todo:
            need = {}
            for s, v in waits:
                if v > seen.get(s, 0) and v > need.get(s, 0):
                    need[s] = v
            for s, v in need.items():
                e.wait_ge(s, v)
                seen[s] = v
            if fn is None:
                continue
            ins = fn(e)
            if sem is not None:
                ins.then_inc(sem, 1)


class Pool:

    def __init__(self, bufs):
        self.free = [(b, ()) for b in bufs]

    def get(self):
        return self.free.pop(0)

    def put(self, buf, *toks):
        self.free.append((buf, toks))


class Operand:

    def __init__(self, t):
        self.t = t
        self.tok = [()] * 16
        self.free = ()

    def hi(self, k, n=1):
        return self.t[:, 0, k * T:(k + n) * T]

    def lo(self, k, n=1):
        return self.t[:, 1, k * T:(k + n) * T]


def build(nc, d, out):
    ctx = ExitStack()
    with ctx:
        def sb(name, shape, dt=F32):
            return ctx.enter_context(nc.sbuf_tensor(name, shape, dt))

        def sem(name):
            return ctx.enter_context(nc.semaphore(name))

        raw = sb("raw", [P, NRAW, UNIT])
        whi = sb("whi", [P, NW, SUB], F32R)
        wlo = sb("wlo", [P, NW, SUB], F32R)
        X = sb("X", [P, 16 * T])
        H = Operand(sb("H", [P, 2, 16 * T], F32R))
        Y = Operand(sb("Y", [P, 2, 16 * T], F32R))
        CR = sb("CR", [P, 896], F32R)
        ADT = sb("ADT", [P, 4, 32], F32R)
        AR = sb("AR", [P, 16896])
        PS = ctx.enter_context(nc.psum_tensor("PS", [P, 8, 512], F32))

        pe, act, dve, pool, sp = (Engine(sem(n)) for n in ("s_pe", "s_act", "s_dve", "s_pool", "s_sp"))
        s_w = [sem(f"s_w{i}") for i in range(NRAW)]
        s_x, s_c, s_v, s_m, s_c2, s_g, s_h, s_out = (sem(n) for n in ("s_x", "s_c", "s_v", "s_m", "s_c2", "s_g", "s_h", "s_out"))

        def xt(k, n=1):
            return X[:, k * T:(k + n) * T]

        G0 = 12288
        vec = AR[:, G0:G0 + NVEC]
        c1 = AR[:, G0 + NVEC:G0 + NVEC + NC1]
        g1 = G0 + NVEC + NC1
        SM = AR[:, g1:g1 + 512]
        g1 += 512
        g_bufs = [AR[:, o:o + 512] for o in range(g1, 16896 - 511, 512)]

        def col(name, i=0):
            o = VOFF[name][0] + i
            return vec[:, o:o + 1]

        def cst(name):
            o, w = C1OFF[name]
            return c1[:, o:o + w]

        ident, tri = cst("ident"), cst("tri")
        ones = tri[:, 128:256]
        TRIr, MNr, Ir = CR[:, 0:384], CR[:, 384:512], CR[:, 512:640]
        sI = [CR[:, 640 + 128 * i:768 + 128 * i] for i in range(2)]

        acc = Pool([PS[:, i, :] for i in range(4)])
        misc = Pool([PS[:, i, :] for i in range(4, 8)])
        tmp = Pool(list(g_bufs))

        order = [(name, i) for name, n in UNITS for i in range(n)]
        n_sub = 2 * len(order)
        hi_tok, lo_tok, done = {}, {}, {}
        state = {"load": 0, "split": 0, "blk": 0}

        def load():
            u = state["load"]
            if u >= len(order):
                return
            state["load"] += 1
            name, i = order[u]
            waits = (lo_tok[2 * (u - NRAW) + 1],) if u >= NRAW else ()
            sp.dma(raw[:, u % NRAW, :], d[name][i], s_w[u % NRAW], *waits)

        def split():
            s = state["split"]
            if s >= n_sub:
                return
            state["split"] += 1
            u = s // 2
            src = raw[:, u % NRAW, (s % 2) * SUB:(s % 2 + 1) * SUB]
            landed = (s_w[u % NRAW], 16 * (u // NRAW + 1))
            used = (done[s - NW],) if s >= NW else ()
            b = s % NW
            hi_tok[s] = act(lambda e: e.activation(whi[:, b, :], src, ACT.Copy), landed, *used)
            lo_tok[s] = dve(lambda e: e.tensor_tensor(wlo[:, b, :], src, whi[:, b, :].bitcast(F32), ALU.subtract),
                            hi_tok[s], landed, *used)
            if s % 2:
                load()

        active, queue = [], []

        def step(width=2):
            while queue and len(active) < width:
                active.append(queue.pop(0))
            for g in list(active):
                try:
                    next(g)
                except StopIteration:
                    active.remove(g)

        def drain():
            while queue or active:
                step()

        def mm(out_, l, r, start, stop, *waits, sig=False):
            return pe(lambda e: e.matmul(out_, l, r, start=start, stop=stop), *waits, sig=sig)

        def block(width, outs, pairs, first, last, waits):
            b = state["blk"]
            s, o = b // 8, (b % 8) * BLK
            state["blk"] = b + width
            ws = (hi_tok[s], lo_tok[s]) + tuple(waits)
            wh, wl = whi[:, s % NW, o:o + width * BLK], wlo[:, s % NW, o:o + width * BLK]
            end = (b + width) % 8 == 0
            tok = None
            for n, (out_, (xh, xl)) in enumerate(zip(outs, pairs)):
                ops = [(wh, xh), (wh, xl), (wl, xh)] if width == 1 else [(xh, wh), (xl, wh), (xh, wl)]
                for i, (l, r) in enumerate(ops):
                    sig = i == 2 and n == len(outs) - 1 and (end or last)
                    tok = mm(out_, l, r, first and i == 0, last and i == 2, *(ws if n == i == 0 else ()), sig=sig)
            if end:
                done[s] = tok
                split()
                step()
            return tok

        def mtiles(op, K, n=2, k0=0):
            bank, free = acc.get()
            for m in range(n):
                for k in range(K):
                    tok = block(1, [bank[:, m * T:(m + 1) * T]], [(op.hi(k0 + k), op.lo(k0 + k))], k == 0, k == K - 1,
                                op.tok[k0 + k] + (free if k == 0 else ()))
            return bank, tok

        def rows(op):
            (b0, f0), (b1, f1) = acc.get(), acc.get()
            for k in range(16):
                tok = block(2, [b0[:, 0:T], b1[:, 0:T]],
                            [(op.hi(k)[:, t * P:(t + 1) * P], op.lo(k)[:, t * P:(t + 1) * P]) for t in range(2)],
                            k == 0, k == 15, op.tok[k] + ((f0 + f1) if k == 0 else ()))
            return (b0, b1), tok

        def halves(op, k, n, src, *waits):
            hi, lo = op.hi(k, n), op.lo(k, n)
            a = act(lambda e: e.activation(hi, src, ACT.Copy), *waits, *op.free)
            b = dve(lambda e: e.tensor_tensor(lo, src, hi.bitcast(F32), ALU.subtract), a, *waits, *op.free)
            for i in range(n):
                op.tok[k + i] = (a, b)
            return b

        def root(dst, ms, scale, eps, *waits):
            a = act(lambda e: e.activation(dst, ms, ACT.Ln, bias=eps, scale=scale), *waits)
            return a, act(lambda e: e.activation(dst, dst, ACT.Exp, scale=-0.5), a)

        class Sum:

            def __init__(self):
                self.buf, self.w = tmp.get()
                self.tok = None

            def add(self, src, *waits):
                if self.tok is None:
                    self.tok = act(lambda e: e.activation(self.buf, src, ACT.Square), *waits, *self.w)
                    return self.tok
                q, w = tmp.get()
                a = act(lambda e: e.activation(q, src, ACT.Square), *waits, *w)
                self.tok = pool(lambda e: e.tensor_tensor(self.buf, self.buf, q, ALU.add), a, self.tok)
                tmp.put(q, self.tok)
                return a

        def finish(s, eps):
            bank, f = misc.get()
            mm(bank[:, 0:T], ones, s.buf[:, 0:T], True, False, s.tok, *f)
            t = mm(bank[:, 0:T], ones, s.buf[:, T:2 * T], False, True, sig=True)
            r, w = tmp.get()
            a, b = root(r[:, 0:T], bank[:, 0:T], 1.0 / 2048, eps, t, *w)
            misc.put(bank, a)
            tmp.put(s.buf, t)
            return r, b

        def apply(src, r, rt, gain, op):
            for k in range(0, 16, 2):
                q, w = tmp.get()
                for i in range(2):
                    c = dve(lambda e, i=i, k=k, q=q: e.scalar_tensor_tensor(
                        q[:, i * T:(i + 1) * T], src(k + i), col(gain, k + i), r[:, 0:T], ALU.mult, ALU.mult), rt, *w)
                tmp.put(q, halves(op, k, 2, q, c))
            tmp.put(r, c)

        act.dma(X[:, :], d["x"], s_x)
        act.dma(vec, d["vec"], s_v)
        act.dma(c1, d["c1"], s_c)
        for _ in range(NRAW):
            load()
        C_OK, V_OK = (s_c, 16), (s_v, 16)
        cr0 = dve(lambda e: e.tensor_copy(CR[:, 0:384], tri), C_OK, V_OK)
        cr1 = dve(lambda e: e.tensor_copy(MNr, cst("mneg")))
        cr2 = dve(lambda e: e.tensor_copy(Ir, ident))
        pool(None, C_OK, V_OK, sig=False)
        pe(None, C_OK, V_OK, cr2, sig=False)
        act(None, C_OK, V_OK, sig=False)

        sx = Sum()
        for k in range(0, 16, 2):
            sx.add(xt(k, 2), (s_x, 16))
        for _ in range(NW):
            split()
        r, rt = finish(sx, col("eps5"))
        dve(None, (s_x, 16), sig=False)
        apply(xt, r, rt, "norm_mix", H)

        mix = [AR[:, o:o + 512] for o in range(9728, G0, 512)]
        for b in mix:
            tmp.put(b)
        Z, XS, CB = AR[:, 0:4096], AR[:, 4096:8192], AR[:, 8192:9728]

        def conv(dst, src, taps, bias, waits, width):
            w = [lambda i=i: taps(i) for i in range(width)]
            last = w[width - 1]()
            if bias is None:
                t = dve(lambda e: e.tensor_scalar(dst[:, 0:T], src[:, 0:T], last, None, ALU.mult), *waits)
            else:
                t = dve(lambda e: e.tensor_scalar(dst[:, 0:T], src[:, 0:T], last, bias, ALU.mult, ALU.add), *waits)
            for sh in range(1, width):
                wi = w[width - 1 - sh]()
                t = dve(lambda e, sh=sh, wi=wi: e.scalar_tensor_tensor(
                    dst[:, sh:T], src[:, 0:T - sh], wi, dst[:, sh:T], ALU.mult, ALU.add), t)
            return t

        def sc_norm(j, v, vt):
            q, w = tmp.get()
            a = act(lambda e: e.activation(q, v, ACT.Square), vt, *w)
            yield
            bank, f = misc.get()
            t = mm(bank, ones, q, True, True, a, *f, sig=True)
            a1, rt = root(q, bank, 1.0 / 128, col("eps5"), t)
            misc.put(bank, a1)
            for i in range(2):
                c = dve(lambda e, i=i: e.scalar_tensor_tensor(
                    v[:, i * T:(i + 1) * T], v[:, i * T:(i + 1) * T], col("sc_norm", 2 * j + i), q[:, i * T:(i + 1) * T],
                    ALU.mult, ALU.mult), rt, vt)
            tmp.put(q, c)
            tmp.put(v, halves(Y, 2 * j, 2, v, c))

        for j in range(8):
            bu, tu = mtiles(H, 16)
            u, w = tmp.get()
            a = act(lambda e, u=u, bu=bu: e.activation(u, bu, ACT.Copy), tu, *w)
            acc.put(bu, a)
            bc, tc = mtiles(H, 16)
            c = dve(lambda e, u=u, bc=bc: e.tensor_tensor(u, bc, u, ALU.mult), tc, a)
            acc.put(bc, c)
            v, w = tmp.get()
            for i in range(2):
                vt = conv(v[:, i * T:(i + 1) * T], u[:, i * T:(i + 1) * T],
                          lambda n, i=i, j=j: col("sc_conv_w", n * 16 + 2 * j + i), None, (c,) + w, 3)
            tmp.put(u, vt)
            bb, tb = mtiles(H, 16)
            vt = dve(lambda e, v=v, bb=bb: e.tensor_tensor(v, bb, v, ALU.mult), tb, vt)
            acc.put(bb, vt)
            queue.append(sc_norm(j, v, vt))

        def xbc(i0, dst, ready, *waits):
            bank, t = mtiles(H, 16)
            q, w = tmp.get()
            for i in range(2):
                ct = conv(q[:, i * T:(i + 1) * T], bank[:, i * T:(i + 1) * T],
                          lambda n, i=i: col("ssd_conv_w", n * 24 + i0 + i), col("ssd_conv_b", i0 + i), (t,) + w, 4)
            acc.put(bank, ct)
            a = act(lambda e: e.activation(dst if dst is not None else q, q, ACT.Silu), ct, *waits)
            if dst is not None:
                tmp.put(q, a)
            return q, a

        for i in range(4):
            _, bc_tok = xbc(16 + 2 * i, Z[:, i * 512:(i + 1) * 512], None)
        BM, CM_ = Z[:, 0:1024], Z[:, 1024:2048]
        cb_tok = [None] * 4

        def cb_task():
            for g in range(4):
                bank, f = misc.get()
                mm(bank[:, 0:256], BM[:, g * T:g * T + 128], CM_[:, g * T:(g + 1) * T], True, True, bc_tok, *f)
                t = mm(bank[:, 256:384], BM[:, g * T + 128:(g + 1) * T], CM_[:, g * T + 128:(g + 1) * T], True, True, sig=True)
                cb_tok[g] = act(lambda e, g=g, bank=bank: e.activation(CB[:, g * 384:(g + 1) * 384], bank[:, 0:384], ACT.Copy), t)
                misc.put(bank, cb_tok[g])
                yield

        queue.append(cb_task())
        bdt, tdt = mtiles(H, 16, 1)
        dtT = SM[:, 0:64]
        nacs = SM[:, 64:128]
        arow = SM[:, 128:160]
        adt = SM[:, 160:224]
        ssd_ready = []

        def dt_task():
            x, w = tmp.get()
            y, w2 = tmp.get()
            xv, ab, e1, u1 = (q[0:32, :] for q in (x[:, 0:T], x[:, T:2 * T], y[:, 0:T], y[:, T:2 * T]))
            c = dve(lambda e: e.tensor_scalar(xv, bdt[0:32, 0:T], col("dt_bias")[0:32, :], None, ALU.add), tdt, *w, *w2)
            acc.put(bdt, c)
            a = act(lambda e: e.activation(ab, xv, ACT.Abs), c)
            a = act(lambda e: e.activation(e1, ab, ACT.Exp, scale=-1.0), a)
            c1_ = dve(lambda e: e.tensor_scalar(u1, e1, 1.0, None, ALU.add), a)
            a = act(lambda e: e.activation(ab, u1, ACT.Ln), c1_)
            yield
            c = dve(lambda e: e.tensor_scalar(u1, u1, -1.0, None, ALU.add), a)
            m, wm = tmp.get()
            mk, rc = m[0:32, 0:T], m[0:32, T:2 * T]
            c = dve(lambda e: e.tensor_scalar(mk, u1, 0.0, None, ALU.is_equal), c, *wm)
            k1 = dve(lambda e: e.tensor_tensor(u1, u1, mk, ALU.add), c)
            k2 = dve(lambda e: e.tensor_tensor(ab, ab, mk, ALU.add), c)
            k3 = dve(lambda e: e.reciprocal(rc, u1), k1)
            k4 = dve(lambda e: e.tensor_tensor(ab, ab, e1, ALU.mult), k2)
            k5 = dve(lambda e: e.tensor_tensor(ab, ab, rc, ALU.mult), k3, k4)
            k6 = dve(lambda e: e.scalar_tensor_tensor(xv, xv, 0.0, ab, ALU.max, ALU.add), k5)
            yield
            bank, f = misc.get()
            for t in range(2):
                tt = pe(lambda e, t=t: e.transpose(bank[:, t * 32:(t + 1) * 32], xv[:, t * P:(t + 1) * P], ident[0:32, 0:32]),
                        k6, *f)
            c = dve(lambda e: e.tensor_copy(dtT, bank[:, 0:64]), tt)
            misc.put(bank, c)
            tmp.put(x, tt)
            tmp.put(y, k6)
            tmp.put(m, k6)
            ar = act(lambda e: e.activation(arow, vec[:, VOFF["a_log"][0]:VOFF["a_log"][0] + 32], ACT.Exp))
            for t in range(2):
                c2 = dve(lambda e, t=t: e.scalar_tensor_tensor(adt[:, t * 32:(t + 1) * 32], dtT[:, t * 32:(t + 1) * 32], -1.0,
                                                                 arow, ALU.mult, ALU.mult), c, ar)
            h = dve(lambda e: e.tensor_copy(ADT[:, 0:2, :], adt), c2)
            l = dve(lambda e: e.tensor_tensor(ADT[:, 2:4, :], adt, ADT[:, 0:2, :].bitcast(F32).rearrange("p a b -> p (a b)"),
                                              ALU.subtract), h)
            yield
            bank, f = misc.get()
            mm(bank[:, 0:32], tri[:, 0:128], adt[:, 0:32], True, True, c2, *f)
            mm(bank[:, 32:64], ones, adt[:, 0:32], True, False)
            t = mm(bank[:, 32:64], tri[:, 0:128], adt[:, 32:64], False, True, sig=True)
            c = dve(lambda e: e.tensor_scalar(nacs, bank[:, 0:64], -1.0, None, ALU.mult), t)
            misc.put(bank, c)
            ssd_ready.extend([c, l])

        queue.append(dt_task())
        xs_tok = [None] * 8

        def xs_task(j, q, a):
            yield
            bank, f = misc.get()
            for t in range(2):
                for i in range(2):
                    tt = pe(lambda e, t=t, i=i: e.transpose(bank[:, t * T + i * P:t * T + (i + 1) * P],
                                                              q[:, i * T + t * P:i * T + (t + 1) * P], ident), a, *f)
            dst = XS.rearrange("p (t n) -> p t n", t=2)[:, :, j * T:(j + 1) * T]
            xs_tok[j] = act(lambda e: e.activation(dst, bank.rearrange("p (t n) -> p t n", t=2), ACT.Copy), tt)
            misc.put(bank, xs_tok[j])
            tmp.put(q, tt)

        for j in range(8):
            q, a = xbc(2 * j, None, None)
            queue.append(xs_task(j, q, a))
        drain()
        z_tok = [None] * 16
        for j in range(8):
            bank, t = mtiles(H, 16)
            a = act(lambda e, j=j, bank=bank: e.activation(Z[:, j * 512:(j + 1) * 512], bank, ACT.Silu), t, *cb_tok)
            acc.put(bank, a)
            z_tok[2 * j] = z_tok[2 * j + 1] = a
        H.free = (t,)

        def ssd_pair(i):
            es = []
            for h in (2 * i, 2 * i + 1):
                g = h // 8
                bank, f = misc.get()
                w0 = [ADT[:, 2 * p, h:h + 1].to_broadcast([P, P]) for p in range(2)]
                w1 = [ADT[:, 2 * p + 1, h:h + 1].to_broadcast([P, P]) for p in range(2)]
                mm(bank[:, 0:384], w0[0], TRIr, True, False, *ssd_ready, *f)
                mm(bank[:, 0:384], w0[1], TRIr, False, False)
                for p in range(2):
                    for o in (128, 256):
                        mm(bank[:, o:o + 128], w1[p], TRIr[:, 0:128], False, False)
                mm(bank[:, 0:128], Ir, MNr, False, False)
                t = mm(bank[:, 256:384], Ir, MNr, False, True, sig=True)
                E, w = tmp.get()
                a0 = act(lambda e, h=h, E=E, bank=bank: e.activation(E[:, 0:256], bank[:, 0:256], ACT.Exp,
                                                                       bias=nacs[:, h:h + 1]), t, *w, *ssd_ready)
                a1 = act(lambda e, h=h, E=E, bank=bank: e.activation(E[:, 256:384], bank[:, 256:384], ACT.Exp,
                                                                       bias=nacs[:, 32 + h:33 + h]))
                misc.put(bank, a1)
                cb = CB[:, g * 384:(g + 1) * 384]
                c0 = dve(lambda e, h=h, E=E, cb=cb: e.scalar_tensor_tensor(
                    E[:, 0:256], cb[:, 0:256], dtT[:, h:h + 1], E[:, 0:256], ALU.mult, ALU.mult), a0, cb_tok[g])
                c1_ = dve(lambda e, h=h, E=E, cb=cb: e.scalar_tensor_tensor(
                    E[:, 256:384], cb[:, 256:384], dtT[:, 32 + h:33 + h], E[:, 256:384], ALU.mult, ALU.mult), a1)
                for o, cc in ((0, c0), (256, c1_)):
                    c = dve(lambda e, h=h, E=E, o=o: e.scalar_tensor_tensor(
                        E[:, o:o + 128], ident, col("d_skip", h), E[:, o:o + 128], ALU.mult, ALU.add), cc)
                es.append((h, E, c))
            yield
            bank, f = misc.get()
            for h, E, c in es:
                o = bank[64 * (h % 2):64 * (h % 2) + 64, 0:T]
                mm(o, XS[:, 64 * h:64 * h + 64], E[:, 0:256], True, False, c, xs_tok[h // 4], *f)
                t = mm(o[:, 128:256], XS[:, 2048 + 64 * h:2048 + 64 * h + 64], E[:, 256:384], False, True, sig=True)
                tmp.put(E, t)
            zt = Z[:, i * T:(i + 1) * T]
            z_tok[i] = dve(lambda e: e.tensor_tensor(zt, bank[:, 0:T], zt, ALU.mult), t, z_tok[i])
            misc.put(bank, z_tok[i])

        def ssd_group(g):
            while any(z_tok[i] in z_silu for i in range(4 * g, 4 * g + 4)):
                yield
            zs = [Z[:, (4 * g + 2 * p) * T:(4 * g + 2 * p + 2) * T] for p in range(2)]
            qs = []
            for p in range(2):
                q, w = tmp.get()
                a = act(lambda e, p=p, q=q: e.activation(q, zs[p], ACT.Square), z_tok[4 * g + 2 * p], z_tok[4 * g + 2 * p + 1], *w)
                qs.append(q)
            yield
            bank, f = misc.get()
            for n in range(4):
                t = mm(bank[:, 0:T], ones, qs[n // 2][:, (n % 2) * T:(n % 2 + 1) * T], n == 0, n == 3, a, *f, sig=n == 3)
            r = qs[0][:, 0:T]
            a1, rt = root(r, bank[:, 0:T], 1.0 / 512, col("eps5"), t)
            misc.put(bank, a1)
            tmp.put(qs[1], t)
            yield
            for p in range(2):
                for i in range(2):
                    k = 4 * g + 2 * p + i
                    c = dve(lambda e, k=k: e.scalar_tensor_tensor(
                        Z[:, k * T:(k + 1) * T], Z[:, k * T:(k + 1) * T], col("ssd_norm", k), r, ALU.mult, ALU.mult),
                        rt, z_tok[k])
                last = halves(H, 4 * g + 2 * p, 2, zs[p], c)
            tmp.put(qs[0], c)
            z_end.append(last)

        z_silu, z_end = set(z_tok), []
        for g in range(4):
            for i in range(4):
                queue.append(ssd_pair(4 * g + i))
            queue.append(ssd_group(g))

        def residual(bank, t, j, s=None, release=acc):
            c = dve(lambda e: e.tensor_tensor(xt(2 * j, 2), xt(2 * j, 2), bank, ALU.add), t)
            release.put(bank, c)
            if s is not None:
                s.add(xt(2 * j, 2), c)

        for j in range(8):
            bank, t = mtiles(Y, 16)
            residual(bank, t, j)
        Y.free = (t,)
        drain()

        act.dma(XS, d["mem"], s_m, t, *[z_tok[i] for i in range(16)])

        def mem_task():
            s = Sum()
            for k in range(0, 16, 2):
                s.add(XS[:, k * T:(k + 2) * T], (s_m, 16))
                if k % 4:
                    yield
            r, rt = finish(s, col("eps5"))
            yield
            dve(None, (s_m, 16), sig=False)
            apply(lambda k: XS[:, k * T:(k + 1) * T], r, rt, "mem_norm", Y)

        queue.append(mem_task())
        sx = Sum()
        for j in range(8):
            bank, t = mtiles(H, 16)
            residual(bank, t, j, sx)
        H.free = (t,)
        drain()

        def norm_task(s, eps, gain, op):
            r, rt = finish(s, col(eps))
            yield
            apply(xt, r, rt, gain, op)

        queue.append(norm_task(sx, "eps5", "norm_xa", H))
        KT, VM, QT = Z[:, 0:1024], Z[:, 1024:2048], Z[:, 2048:3072]
        for j in range(2):
            bank, t = mtiles(Y, 16)
            k_tok = act(lambda e, j=j, bank=bank: e.activation(KT[:, j * 512:(j + 1) * 512], bank, ACT.Copy), t, *z_end)
            acc.put(bank, k_tok)
        for j in range(2):
            banks, t = rows(Y)
            for m in range(2):
                v_tok = act(lambda e, j=j, m=m, b=banks[m]: e.activation(
                    VM[:, m * 512 + j * T:m * 512 + (j + 1) * T], b[:, 0:T], ACT.Copy), t)
                acc.put(banks[m], v_tok)
        Y.free = (t,)
        drain()
        for j in range(2):
            bank, t = mtiles(H, 16)
            q_tok = act(lambda e, j=j, bank=bank: e.activation(QT[:, j * 512:(j + 1) * 512], bank, ACT.Copy,
                                                                 scale=128.0 ** -0.5), t)
            acc.put(bank, q_tok)
        H.free = (t,)
        stat = SM[:, 224:512]

        def xa_head(h):
            st = stat[:, 8 * h:8 * h + 8]
            bank, f = misc.get()
            for t in range(2):
                tt = mm(bank[:, t * T:(t + 1) * T], QT[:, h * T + t * P:h * T + (t + 1) * P], KT[:, h * T:(h + 1) * T],
                        True, True, q_tok, k_tok, *f, sig=t == 1)
            c = dve(lambda e: e.tensor_reduce(st[:, 0:2], bank.rearrange("p (t n) -> p t n", t=2), AX, ALU.max, negate=True), tt)
            Pb, w = tmp.get()
            for t in range(2):
                a = act(lambda e, t=t: e.activation(Pb[:, t * T:(t + 1) * T], bank[:, t * T:(t + 1) * T], ACT.Exp,
                                                     bias=st[:, t:t + 1], accum_out=st[:, 2 + t:3 + t]), c, *w)
            misc.put(bank, a)
            c = dve(lambda e: e.reciprocal(st[:, 4:6], st[:, 2:4]), a)
            for t in range(2):
                cn = dve(lambda e, t=t: e.tensor_scalar(Pb[:, t * T:(t + 1) * T], Pb[:, t * T:(t + 1) * T],
                                                        st[:, 4 + t:5 + t], None, ALU.mult), c)
            yield
            bank, f = misc.get()
            for m in range(2):
                for t in range(2):
                    tt = pe(lambda e, m=m, t=t: e.transpose(bank[:, m * T + t * P:m * T + (t + 1) * P],
                                                              Pb[:, t * T + m * P:t * T + (m + 1) * P], ident), cn, *f)
            PT, w = tmp.get()
            a = act(lambda e: e.activation(PT, bank, ACT.Copy), tt, *w)
            misc.put(bank, a)
            tmp.put(Pb, tt)
            yield
            bank, f = misc.get()
            for m in range(2):
                tt = mm(bank[:, 0:T], VM[:, m * 512 + h * P:m * 512 + (h + 1) * P], PT[:, m * T:(m + 1) * T],
                        m == 0, m == 1, a, v_tok, *f, sig=m == 1)
            tmp.put(PT, tt)
            misc.put(bank, halves(Y, h, 1, bank[:, 0:T], tt))

        for h in range(4):
            queue.append(xa_head(h))
        drain()
        c2_free = [t for b, toks in tmp.free if any(b is m for m in mix) for t in toks]
        tmp.free = [x for x in tmp.free if not any(x[0] is m for m in mix)]
        sx = Sum()
        for j in range(8):
            bank, t = mtiles(Y, 4)
            residual(bank, t, j, sx)
        Y.free = (t,)

        def ffn(conv2):
            s = None
            for a0, a1 in PARTS:
                for j in range(a0, a1, 2):
                    bg, tg = mtiles(H, 16)
                    q, w = tmp.get()
                    if conv2:
                        for i in range(2):
                            tg = conv(q[:, i * T:(i + 1) * T], bg[:, i * T:(i + 1) * T],
                                      lambda n, i=i, j=j: col("conv_w_2", n * 44 + j + i), col("conv_b_2", j + i), (tg,) + w, 3)
                        acc.put(bg, tg)
                        a = act(lambda e, q=q: e.activation(q, q, ACT.Silu), tg)
                    else:
                        a = act(lambda e, q=q, bg=bg: e.activation(q, bg, ACT.Silu), tg, *w)
                        acc.put(bg, a)
                    bu, tu = mtiles(H, 16)
                    c = dve(lambda e, q=q, bu=bu: e.tensor_tensor(q, bu, q, ALU.mult), tu, a)
                    acc.put(bu, c)
                    tmp.put(q, halves(Y, j - a0, 2, q, c))
                if a1 == 44:
                    H.free = (tu,)
                    s = Sum()
                for j in range(8):
                    bank, t = mtiles(Y, a1 - a0)
                    residual(bank, t, j, s)
                Y.free = (t,)
            return s

        for _ in norm_task(sx, "eps5", "norm_ffn", H):
            pass
        sx = ffn(False)

        def in_place(s, eps, gain):
            r, rt = finish(s, col(eps))
            for k in range(16):
                c = dve(lambda e, k=k: e.scalar_tensor_tensor(xt(k), xt(k), col(gain, k), r[:, 0:T], ALU.mult, ALU.mult), rt)
                yield k, c
            tmp.put(r, c)

        c2 = AR[:, 9216:9216 + NC2]
        act.dma(c2, d["c2"], s_c2, *c2_free)
        for o in (9216 + NC2, 9216 + NC2 + 512):
            tmp.put(AR[:, o:o + 512])

        def k2(name):
            o, w = C2OFF[name]
            return c2[:, o:o + w]

        bank, f = misc.get()
        for k, c in in_place(sx, "eps5", "norm_final"):
            if k % 2:
                q, w = tmp.get()
                a = act(lambda e, q=q, k=k: e.activation(q, xt(k - 1, 2), ACT.Square), c, *w)
                for i in range(2):
                    t = mm(bank[:, 0:T], ones, q[:, i * T:(i + 1) * T], k == 1 and i == 0, k == 15 and i == 1, a, *f,
                           sig=i == 1)
                tmp.put(q, t)
        r, w = tmp.get()
        a, rt = root(r[:, 0:T], bank[:, 0:T], 1.0 / 2048, col("eps6"), t, *w)
        misc.put(bank, a)
        apply(xt, r, rt, "attn_norm_2", H)
        C2_OK = (s_c2, 16)
        dve(None, C2_OK, sig=False)
        pe(None, C2_OK, sig=False)

        lam = SM[:, 0:16]
        lv = k2("lam")
        Dr, MCr = CR[:, 0:384], CR[:, 384:448]
        dr_tok = dve(lambda e: e.tensor_copy(Dr, k2("dist")))
        mc_tok = dve(lambda e: e.tensor_copy(MCr, k2("mc")))
        q, w = tmp.get()
        for i in range(2):
            c = dve(lambda e, i=i, q=q: e.tensor_tensor(q[:, 64 * i:64 * i + 64], lv[:, 128 * i:128 * i + 64],
                                                        lv[:, 128 * i + 64:128 * i + 128], ALU.mult), *w)
        c = dve(lambda e: e.tensor_reduce(lam[:, 0:2], q[:, 0:128].rearrange("p (a b) -> p a b", a=2), AX, ALU.add), c)
        tmp.put(q, c)
        a = act(lambda e: e.activation(lam[:, 2:4], lam[:, 0:2], ACT.Exp), c)
        c = dve(lambda e: e.tensor_tensor(lam[:, 4:5], lam[:, 2:3], lam[:, 3:4], ALU.subtract), a)
        c = dve(lambda e: e.tensor_scalar(lam[:, 4:5], lam[:, 4:5], 0.8 - 0.6, None, ALU.add), c)
        c = dve(lambda e: e.tensor_scalar(lam[:, 5:6], lam[:, 4:5], -1.0, None, ALU.mult), c)
        c = dve(lambda e: e.tensor_tensor(lam[:, 6:7], lam[:, 4:5], lam[:, 5:6], ALU.max), c)
        c = dve(lambda e: e.tensor_scalar(lam[:, 6:7], lam[:, 6:7], 1.0, None, ALU.max), c)
        c = dve(lambda e: e.reciprocal(lam[:, 7:8], lam[:, 6:7]), c)
        c0 = dve(lambda e: e.tensor_tensor(lam[:, 8:9], lam[:, 5:6], lam[:, 7:8], ALU.mult), c)
        c1_ = dve(lambda e: e.tensor_tensor(lam[:, 9:10], lam[:, 7:8], lam[:, 7:8], ALU.mult), c)
        c1_ = dve(lambda e: e.tensor_scalar(lam[:, 9:10], lam[:, 9:10], 1e-5, None, ALU.mult), c1_)
        c2_ = dve(lambda e: e.tensor_scalar(lam[:, 10:11], col("diff_subln_2"), 1.0 - (0.8 - 0.6), None, ALU.mult))
        lam_ok = (c0, c1_, c2_)
        inv, nlam, eps_a, gain_a = lam[:, 7:8], lam[:, 8:9], lam[:, 9:10], lam[:, 10:11]

        base = 9216
        G_row, gw = tmp.get()
        g8 = G_row[0:8, :]
        act.dma(g8[:, 127:319], d["rel"], s_g, *gw)
        c = dve(lambda e: e.tensor_copy(g8[:, 0:127], g8[:, 127:128].to_broadcast([8, 127])), (s_g, 16), *gw)
        c = dve(lambda e: e.tensor_copy(g8[:, 319:511], g8[:, 318:319].to_broadcast([8, 192])))
        c = dve(lambda e: e.tensor_copy(g8[:, 511:512], g8[:, 318:319]))
        scratch = nc.dram_tensor("rel_rows", [8, 512], F32).ap()
        act.dma(scratch, g8, s_g, c)
        hank_src = bass.AP(tensor=scratch.tensor, offset=0, ap=[[1, P], [512, 8], [1, 256]])
        tmp.put(G_row, (s_g, 32))

        QA, KA, VA = AR[:, 0:2048], AR[:, 2048:4096], AR[:, 4096:6144]
        QB, KB, VB = AR[:, 6144:7168], AR[:, 7168:8192], AR[:, 8192:9216]
        QC, KC, VC = AR[:, 0:1024], AR[:, 1024:2048], AR[:, 2048:3072]
        HK = AR[:, 3072:5120]

        def qkv(dq, dk, dv, n, *waits):
            toks = []
            for dst, sc in ((dq, 0.125), (dk, 1.0)):
                for j in range(n // 2):
                    bank, t = mtiles(H, 16)
                    a = act(lambda e, j=j, bank=bank, dst=dst, sc=sc: e.activation(
                        dst[:, j * 512:(j + 1) * 512], bank, ACT.Copy, scale=sc), t, *waits)
                    acc.put(bank, a)
            for j in range(n // 2):
                banks, t = rows(H)
                for m in range(2):
                    a = act(lambda e, j=j, m=m, b=banks[m]: e.activation(
                        dv[:, m * n * P + j * T:m * n * P + (j + 1) * T], b[:, 0:T], ACT.Copy), t, *waits)
                    acc.put(banks[m], a)
            return a, t

        a_tok, t = qkv(QA, KA, VA, 8)

        def scaled(o_bank, tt, mat, scale, eps, gain, tile, *waits):
            q, w = tmp.get()
            a = act(lambda e: e.activation(q[:, 0:T], o_bank[:, 0:T], ACT.Square), tt, *w, *waits)
            yield
            bank, f = misc.get()
            t = mm(bank[:, 0:T], mat, q[:, 0:T], True, True, a, *f, sig=True)
            a1, rt = root(q[:, T:2 * T], bank[:, 0:T], scale, eps, t)
            misc.put(bank, a1)
            yield
            c = dve(lambda e: e.scalar_tensor_tensor(q[:, 0:T], o_bank[:, 0:T], gain, q[:, T:2 * T], ALU.mult, ALU.mult), rt)
            misc.put(o_bank, c)
            tmp.put(q, halves(Y, tile, 1, q[:, 0:T], c))

        def turn(Wb, wt):
            bank, f = misc.get()
            for o, s in ((0, 0), (128, 128), (256, 256)):
                tt = pe(lambda e, o=o, s=s: e.transpose(bank[:, o:o + 128], Wb[:, s:s + 128], ident), wt, *f)
            WT, w = tmp.get()
            a = act(lambda e: e.activation(WT[:, 0:384], bank[:, 0:384], ACT.Copy), tt, *w)
            misc.put(bank, a)
            tmp.put(Wb, tt)
            return WT, a

        def diff_head(h):
            st = SM[:, 32 + 16 * (h % 4):48 + 16 * (h % 4)]
            si = dve(lambda e: e.tensor_scalar(sI[h % 2], ident, 2.0 ** -(h + 1), None, ALU.mult), *si_free[h % 2])
            Ps = []
            for c in range(2):
                bank, f = misc.get()
                lo_, hi_ = 64 * c, 64 * c + 64
                mm(bank[:, 0:384], sI[h % 2], Dr, True, False, si, dr_tok, *f)
                mm(bank[:, 0:128], QA[lo_:hi_, h * T:h * T + 128], KA[lo_:hi_, h * T:h * T + 128], False, False, a_tok)
                tt = mm(bank[:, 128:384], QA[lo_:hi_, h * T + 128:(h + 1) * T], KA[lo_:hi_, h * T:(h + 1) * T],
                        False, True, sig=True)
                for o, n, i in ((0, 128, 0), (128, 256, 1)):
                    cm = dve(lambda e, o=o, n=n, i=i, bank=bank, c=c: e.tensor_reduce(
                        st[:, 2 * c + i:2 * c + i + 1], bank[:, o:o + n], AX, ALU.max, negate=True), tt)
                Pb, w = tmp.get()
                for o, n, i in ((0, 128, 0), (128, 256, 1)):
                    a = act(lambda e, o=o, n=n, i=i, bank=bank, c=c, Pb=Pb: e.activation(
                        Pb[:, o:o + n], bank[:, o:o + n], ACT.Exp, bias=st[:, 2 * c + i:2 * c + i + 1],
                        accum_out=st[:, 4 + 2 * c + i:5 + 2 * c + i]), cm, *w)
                misc.put(bank, a)
                Ps.append(Pb)
            si_free[h % 2] = (tt,)
            r = dve(lambda e: e.reciprocal(st[:, 8:12], st[:, 4:8]), a)
            r0 = dve(lambda e: e.tensor_scalar(st[:, 8:10], st[:, 8:10], inv, None, ALU.mult), r, *lam_ok)
            r1 = dve(lambda e: e.tensor_scalar(st[:, 10:12], st[:, 10:12], nlam, None, ALU.mult), r)
            for o, n, i in ((0, 128, 0), (128, 256, 1)):
                m = dve(lambda e, o=o, n=n, i=i: e.tensor_scalar(Ps[1][:, o:o + n], Ps[1][:, o:o + n],
                                                                 st[:, 10 + i:11 + i], None, ALU.mult), r1)
                wt = dve(lambda e, o=o, n=n, i=i: e.scalar_tensor_tensor(
                    Ps[0][:, o:o + n], Ps[0][:, o:o + n], st[:, 8 + i:9 + i], Ps[1][:, o:o + n], ALU.mult, ALU.add), m, r0)
            tmp.put(Ps[1], wt)
            yield
            WT, a = turn(Ps[0], wt)
            yield
            bank, f = misc.get()
            mm(bank[:, 0:T], VA[:, h * P:(h + 1) * P], WT[:, 0:256], True, False, a, a_tok, *f)
            tt = mm(bank[:, 128:256], VA[:, 1024 + h * P:1024 + (h + 1) * P], WT[:, 256:384], False, True, sig=True)
            tmp.put(WT, tt)
            pv_tok.append(tt)
            yield from scaled(bank, tt, ones, 1.0 / 128, eps_a, gain_a, h, *lam_ok)

        si_free = [(cr2,), (cr2,)]
        pv_tok = []
        for h in range(8):
            queue.append(diff_head(h))
        b_tok, t = qkv(QB, KB, VB, 4)
        drain()
        hk = [pv_tok[-1], pv_tok[-2], (s_g, 32)]
        act.dma(HK.rearrange("p (h n) -> p h n", h=8), hank_src, s_h, *hk)
        NM, CMk, TRI2, BD, J = k2("nm"), k2("cm"), k2("tri2"), k2("bd"), k2("flip")

        def stick_pair(i):
            o_bank = None
            for h in (2 * i, 2 * i + 1):
                lo_, hi_ = 64 * (h % 2), 64 * (h % 2) + 64
                bank, f = misc.get()
                mm(bank[:, 0:256], KB[lo_:hi_, i * T:i * T + 128], QB[lo_:hi_, i * T:(i + 1) * T], True, True, b_tok, *f)
                tt = mm(bank[:, 256:384], KB[lo_:hi_, i * T + 128:(i + 1) * T], QB[lo_:hi_, i * T + 128:(i + 1) * T],
                        True, True, sig=True)
                z, w = tmp.get()
                q, w2 = tmp.get()
                z_, q_ = z[:, 0:384], q[:, 0:384]
                zc = dve(lambda e, bank=bank, z_=z_: e.tensor_tensor(z_, bank[:, 0:384], CMk, ALU.mult), tt, *w)
                misc.put(bank, zc)
                a = act(lambda e, z_=z_, q_=q_: e.activation(q_, z_, ACT.Abs), zc, *w2)
                a = act(lambda e, q_=q_: e.activation(q_, q_, ACT.Exp, scale=-1.0), a)
                a = act(lambda e, q_=q_: e.activation(q_, q_, ACT.Ln, bias=1.0), a)
                c = dve(lambda e, z_=z_, q_=q_: e.scalar_tensor_tensor(q_, z_, 0.0, q_, ALU.max, ALU.add), a)
                c = dve(lambda e, q_=q_: e.tensor_tensor(q_, q_, NM, ALU.mult), c)
                yield
                bank, f = misc.get()
                mm(bank[:, 0:256], TRI2, q[:, 0:256], True, False, c, *f)
                mm(bank[:, 128:256], ones, q[:, 256:384], False, True)
                tt = mm(bank[:, 256:384], TRI2, q[:, 256:384], True, True, sig=True)
                tmp.put(q, tt)
                c = dve(lambda e, bank=bank, z_=z_: e.tensor_tensor(z_, bank[:, 0:384], z_, ALU.add), tt)
                misc.put(bank, c)
                a = act(lambda e, z_=z_: e.activation(z_, z_, ACT.Exp), c)
                c = dve(lambda e, z_=z_: e.tensor_tensor(z_, z_, CMk, ALU.mult), a)
                yield
                if o_bank is None:
                    o_bank, f = misc.get()
                else:
                    f = ()
                o = o_bank[lo_:hi_, 0:T]
                mm(o, VB[:, h * 64:h * 64 + 64], z[:, 0:256], True, False, c, *f)
                tt = mm(o[:, 128:256], VB[:, 512 + h * 64:512 + h * 64 + 64], z[:, 256:384], False, True, sig=True)
                tmp.put(z, tt)
            yield from scaled(o_bank, tt, BD, 1.0 / 64, col("eps6"), col("sb_norm_2", i), 8 + i)

        def band_pair(i):
            o_bank = None
            for h in (2 * i, 2 * i + 1):
                lo_, hi_ = 64 * (h % 2), 64 * (h % 2) + 64
                st = SM[:, 96 + 16 * (h % 4):112 + 16 * (h % 4)]
                bank, f = misc.get()
                hk_ = HK[:, h * T:(h + 1) * T]
                mm(bank[:, 0:128], J, hk_[:, 128:256], True, False, (s_h, 16), *f)
                mm(bank[:, 0:128], QC[lo_:hi_, i * T:i * T + 128], KC[lo_:hi_, i * T:i * T + 128], False, False, c_tok)
                mm(bank[:, 64:128], Ir, MCr, False, True, mc_tok)
                mm(bank[:, 128:384], J, hk_, True, False)
                mm(bank[:, 128:384], QC[lo_:hi_, i * T + 128:(i + 1) * T], KC[lo_:hi_, i * T:(i + 1) * T], False, False)
                tt = mm(bank[:, 320:384], Ir, MCr, False, True, sig=True)
                for o, n, k in ((0, 128, 0), (128, 256, 1)):
                    cm = dve(lambda e, o=o, n=n, k=k, bank=bank, st=st: e.tensor_reduce(
                        st[:, k:k + 1], bank[:, o:o + n], AX, ALU.max, negate=True), tt)
                Pb, w = tmp.get()
                for o, n, k in ((0, 128, 0), (128, 256, 1)):
                    a = act(lambda e, o=o, n=n, k=k, bank=bank, Pb=Pb, st=st: e.activation(
                        Pb[:, o:o + n], bank[:, o:o + n], ACT.Exp, bias=st[:, k:k + 1], accum_out=st[:, 2 + k:3 + k]), cm, *w)
                misc.put(bank, a)
                r = dve(lambda e, st=st: e.reciprocal(st[:, 4:6], st[:, 2:4]), a)
                for o, n, k in ((0, 128, 0), (128, 256, 1)):
                    wt = dve(lambda e, o=o, n=n, k=k, Pb=Pb, st=st: e.tensor_scalar(
                        Pb[:, o:o + n], Pb[:, o:o + n], st[:, 4 + k:5 + k], None, ALU.mult), r)
                yield
                WT, a = turn(Pb, wt)
                yield
                if o_bank is None:
                    o_bank, f = misc.get()
                else:
                    f = ()
                o = o_bank[lo_:hi_, 0:T]
                mm(o, VC[:, h * 64:h * 64 + 64], WT[:, 0:256], True, False, a, *f)
                tt = mm(o[:, 128:256], VC[:, 512 + h * 64:512 + h * 64 + 64], WT[:, 256:384], False, True, sig=True)
                tmp.put(WT, tt)
            yield from scaled(o_bank, tt, BD, 1.0 / 64, col("eps6"), col("ch_norm_2", i), 12 + i)

        for i in range(4):
            queue.append(stick_pair(i))
        c_tok, t = qkv(QC, KC, VC, 4, *pv_tok[-2:])
        H.free = (t,)
        for i in range(4):
            queue.append(band_pair(i))
        for j in range(8):
            bank, t = mtiles(Y, 8)
            residual(bank, t, j)
        drain()
        sx = Sum()
        for j in range(8):
            bank, t = mtiles(Y, 8, 2, 8)
            residual(bank, t, j, sx)
        Y.free = (t,)
        for _ in norm_task(sx, "eps6", "ffn_norm_2", H):
            pass
        sx = ffn(True)
        outs = 0
        for k, c in in_place(sx, "eps6", "final_norm_2"):
            if k % 4 == 3:
                sp.dma(out[:, (k - 3) * T:(k + 1) * T], xt(k - 3, 4), s_out, c)
                outs += 16
        sp(None, (s_out, outs), (s_g, 32), (s_h, 16), sig=False)
        assert state["blk"] == 16 * len(order), (state, len(order))

        with nc.Block() as blk:
            @blk.sync
            def _(e):
                sp.play(e)

            @blk.scalar
            def _(e):
                act.play(e)

            @blk.vector
            def _(e):
                dve.play(e)

            @blk.gpsimd
            def _(e):
                pool.play(e)

            @blk.tensor
            def _(e):
                pe.play(e)


def tiles(w):
    k, n = w.shape
    return w.reshape(k // P, P, n // P, P).transpose(2, 0, 1, 3).reshape(-1, P, P)


def wide(w):
    k, n = w.shape
    return w.reshape(k // P, P, n // T, 2, P).transpose(2, 0, 3, 1, 4).reshape(-1, P, P)


def units(*blocks):
    b = np.concatenate(blocks)
    return np.ascontiguousarray(b.reshape(-1, 16, P, P).transpose(0, 2, 1, 3)).reshape(-1, P, UNIT)


def pairs(*ws):
    n = ws[0].shape[1]
    return [tiles(w[:, c:c + T]) for c in range(0, n, T) for w in ws]


def ffn_units(gate, up, down):
    out = []
    for a0, a1 in PARTS:
        out += pairs(gate[:, a0 * P:a1 * P], up[:, a0 * P:a1 * P])
        out.append(tiles(down[a0 * P:a1 * P]))
    return units(*out)


def columns(v):
    return np.ascontiguousarray(v.reshape(-1, P).T)


def layout(a):
    f = np.float32
    w = a["w_in"][0]
    z, xs, bc = w[:, 0:2048], w[:, 2048:4096], w[:, 4096:5120]
    dt = np.concatenate([w[:, 5120:5152], np.zeros((2048, 96), f)], axis=1)
    su, sb_, sc = w[:, 5152:7200], w[:, 7200:9248], w[:, 9248:11296]
    d = {}
    d["w_in"] = units(*pairs(su, sc, sb_), tiles(bc), tiles(dt), tiles(xs), tiles(z))
    d["w_out"] = units(tiles(a["w_out"][0][2048:]), tiles(a["w_out"][0][:2048]))
    d["w_k"], d["w_v"], d["w_q"] = units(tiles(a["w_k"][0])), units(wide(a["w_v"][0])), units(tiles(a["w_q"][0]))
    d["w_o"] = units(tiles(a["w_o"][0]))
    d["ffn"] = ffn_units(a["w_gate"][0], a["w_up"][0], a["w_down"][0])
    q = a["w_qkv_2"][0]
    parts, at = [], 0
    for n in (1024, 512, 512):
        parts += [tiles(q[:, at:at + 2 * n]), wide(q[:, at + 2 * n:at + 3 * n])]
        at += 3 * n
    d["w_qkv_2"] = units(*parts)
    d["w_o_2"] = units(tiles(a["w_o_2"][0][:1024]), tiles(a["w_o_2"][0][1024:]))
    d["ffn_2"] = ffn_units(a["w_gate_2"][0], a["w_up_2"][0], a["w_down_2"][0])

    def fm(x):
        return np.ascontiguousarray(x.reshape(T, 16, P).transpose(2, 1, 0)).reshape(P, 16 * T)

    d["x"], d["mem"] = fm(a["x"]), fm(a["mem"])
    vec = np.zeros((P, NVEC), f)
    for name, (o, n) in VOFF.items():
        if name in ("a_log", "d_skip"):
            v = np.broadcast_to(a[name].reshape(1, 32), (P, 32))
        elif name == "dt_bias":
            v = np.concatenate([a[name].reshape(32), np.zeros(96, f)]).reshape(P, 1)
        elif name in ("eps5", "eps6"):
            v = np.full((P, 1), 1e-5 if name == "eps5" else 1e-6, f)
        else:
            v = columns(a[name])
        vec[:, o:o + n] = v
    d["vec"] = vec
    i = np.arange(P)
    le = (i[:, None] <= i[None, :]).astype(f)
    one = np.ones((P, P), f)
    d["c1"] = np.concatenate([np.eye(P, dtype=f), le, one, one, np.where(le > 0, 0, NEG).astype(f)], axis=1)
    lt = (i[:, None] < i[None, :]).astype(f)
    cm = np.concatenate([lt, one, lt], axis=1)
    qi, ki = i[:, None], np.arange(T)[None, :]
    d0 = np.where(ki[:, :P] // 64 <= qi // 64, -np.abs(qi - ki[:, :P]), NEG)
    d1 = np.where(ki // 64 <= (qi + P) // 64, -np.abs(qi + P - ki), NEG)
    mc = np.where(np.broadcast_to(qi < 64, (P, 64)), NEG, 0.0)
    lam = np.concatenate([a[n].reshape(1, 64) for n in ("lambda_q1_2", "lambda_k1_2", "lambda_q2_2", "lambda_k2_2")], axis=1)
    bd = (i[:, None] // 64 == i[None, :] // 64).astype(f)
    d["c2"] = np.concatenate([bd, le.T, np.eye(P, dtype=f)[::-1], -cm, cm, d0, d1, mc, np.broadcast_to(lam, (P, 256))],
                             axis=1).astype(f)
    d["rel"] = np.ascontiguousarray(a["rel_bias_2"][0][:, ::-1])
    return d


def kernel(**inputs):
    import concourse.bacc as _bacc
    from concourse import mybir as _mybir
    from concourse.bass_utils import run_bass_kernel_spmd as _run

    d = layout({k: np.asarray(v) for k, v in inputs.items()})
    nc = _bacc.Bacc("TRN2", target_bir_lowering=False, num_devices=1)
    arrays, aps = {}, {}
    for name, v in d.items():
        arrays[f"in_{name}"] = v
        aps[name] = nc.dram_tensor(f"in_{name}", v.shape, _mybir.dt.float32, kind="ExternalInput").ap()
    out = nc.dram_tensor("out_0", [P, 16 * T], _mybir.dt.float32, kind="ExternalOutput").ap()
    build(nc, aps, out)
    r = _run(nc, [arrays], core_ids=[0])
    y = r.results[0]["out_0"]
    return np.ascontiguousarray(y.reshape(P, 16, T).transpose(2, 1, 0)).reshape(1, T, 16 * P)
```

```python
from contextlib import ExitStack

import numpy as np

import concourse.bass as bass
from concourse import mybir

F32 = mybir.dt.float32
F32R = mybir.dt.float32r
ALU = mybir.AluOpType
ACT = mybir.ActivationFunctionType
AX = mybir.AxisListType.X

P = 128
T = 256
BLK = 128
SUB = 8 * BLK
UNIT = 2 * SUB
NRAW = 3
NW = 4
NEG = -1e30

PARTS = [(0, 16), (16, 32), (32, 44)]

VEC = [
    ("norm_mix", 16), ("ssd_conv_w", 96), ("ssd_conv_b", 24), ("sc_conv_w", 48), ("sc_norm", 16),
    ("ssd_norm", 16), ("norm_xa", 16), ("mem_norm", 16), ("norm_ffn", 16), ("norm_final", 16),
    ("attn_norm_2", 16), ("diff_subln_2", 1), ("sb_norm_2", 4), ("ch_norm_2", 4), ("ffn_norm_2", 16),
    ("conv_w_2", 132), ("conv_b_2", 44), ("final_norm_2", 16), ("dt_bias", 1), ("a_log", 32),
    ("d_skip", 32), ("eps5", 1), ("eps6", 1),
]
VOFF = {}
_o = 0
for _n, _w in VEC:
    VOFF[_n] = (_o, _w)
    _o += _w
NVEC = _o

C1 = [("ident", 128), ("tri", 384), ("mneg", 128)]
C2 = [("bd", 128), ("tri2", 128), ("flip", 128), ("nm", 384), ("cm", 384), ("dist", 384), ("mc", 64), ("lam", 256)]
C2_KEPT = 1152


def offsets(table):
    out, at = {}, 0
    for name, w in table:
        out[name] = (at, w)
        at += w
    return out, at


C1OFF, NC1 = offsets(C1)
C2OFF, NC2 = offsets(C2)

UNITS = [("w_in", 89), ("w_out", 32), ("w_q", 4), ("w_k", 4), ("w_v", 4), ("w_o", 4), ("ffn", 132),
         ("w_qkv_2", 48), ("w_o_2", 16), ("ffn_2", 132)]


class Bound:

    def matmul(self, *a, **k):
        return lambda e: e.matmul(*a, **k)

    def transpose(self, *a, **k):
        return lambda e: e.transpose(*a, **k)

    def activation(self, *a, **k):
        return lambda e: e.activation(*a, **k)

    def tensor_tensor(self, *a, **k):
        return lambda e: e.tensor_tensor(*a, **k)

    def tensor_scalar(self, *a, **k):
        return lambda e: e.tensor_scalar(*a, **k)

    def scalar_tensor_tensor(self, *a, **k):
        return lambda e: e.scalar_tensor_tensor(*a, **k)

    def tensor_reduce(self, *a, **k):
        return lambda e: e.tensor_reduce(*a, **k)

    def tensor_copy(self, *a, **k):
        return lambda e: e.tensor_copy(*a, **k)

    def reciprocal(self, *a, **k):
        return lambda e: e.reciprocal(*a, **k)


BOUND = Bound()


class Engine:

    def __init__(self, sem):
        self.sem, self.n, self.todo = sem, 0, []

    def __call__(self, fn, *waits, sig=True):
        if sig:
            self.n += 1
        self.todo.append((waits, fn and fn(BOUND), self.sem if sig else None))
        return (self.sem, self.n)

    def dma(self, out, in_, sem, *waits):
        self.todo.append((waits, lambda e: e.dma_start(out, in_).then_inc(sem, 16), None))

    def play(self, e):
        seen = {}
        for waits, fn, sem in self.todo:
            need = {}
            for s, v in waits:
                if v > seen.get(s, 0) and v > need.get(s, 0):
                    need[s] = v
            for s, v in need.items():
                e.wait_ge(s, v)
                seen[s] = v
            if fn is None:
                continue
            ins = fn(e)
            if sem is not None:
                ins.then_inc(sem, 1)


class Pool:

    def __init__(self, bufs):
        self.free = [(b, ()) for b in bufs]

    def get(self):
        return self.free.pop(0)

    def put(self, buf, *toks):
        self.free.append((buf, toks))


class Operand:

    def __init__(self, t):
        self.t = t
        self.tok = [()] * 16
        self.free = ()

    def hi(self, k, n=1):
        return self.t[:, 0, k * T:(k + n) * T]

    def lo(self, k, n=1):
        return self.t[:, 1, k * T:(k + n) * T]


def build(nc, d, out):
    ctx = ExitStack()
    with ctx:
        def sb(name, shape, dt=F32):
            return ctx.enter_context(nc.sbuf_tensor(name, shape, dt))

        def sem(name):
            return ctx.enter_context(nc.semaphore(name))

        raw = sb("raw", [P, NRAW, UNIT])
        whi = sb("whi", [P, NW, SUB], F32R)
        wlo = sb("wlo", [P, NW, SUB], F32R)
        X = sb("X", [P, 16 * T])
        H = Operand(sb("H", [P, 2, 16 * T], F32R))
        Y = Operand(sb("Y", [P, 2, 16 * T], F32R))
        CR = sb("CR", [P, 896], F32R)
        ADT = sb("ADT", [P, 4, 32], F32R)
        AR = sb("AR", [P, 17152])
        PS = ctx.enter_context(nc.psum_tensor("PS", [P, 8, 512], F32))

        pe, act, dve, pool, sp = (Engine(sem(n)) for n in ("s_pe", "s_act", "s_dve", "s_pool", "s_sp"))
        s_w = [sem(f"s_w{i}") for i in range(NRAW)]
        s_x = [sem(f"s_x{i}") for i in range(4)]
        s_c, s_v, s_m, s_c2, s_g, s_h, s_out = (sem(n) for n in ("s_c", "s_v", "s_m", "s_c2", "s_g", "s_h", "s_out"))

        def xt(k, n=1):
            return X[:, k * T:(k + n) * T]

        G0 = 12288
        vec = AR[:, G0:G0 + NVEC]
        c1 = AR[:, G0 + NVEC:G0 + NVEC + NC1]
        g1 = G0 + NVEC + NC1
        SM = AR[:, g1:g1 + 512]
        g1 += 512
        g_bufs = [AR[:, o:o + 512] for o in range(g1, 16896 - 511, 512)]

        def col(name, i=0):
            o = VOFF[name][0] + i
            return vec[:, o:o + 1]

        def cst(name):
            o, w = C1OFF[name]
            return c1[:, o:o + w]

        ident, tri = cst("ident"), cst("tri")
        ones = tri[:, 128:256]
        TRIr, MNr, Ir = CR[:, 0:384], CR[:, 384:512], CR[:, 512:640]
        sI = [CR[:, 640 + 128 * i:768 + 128 * i] for i in range(2)]

        acc = Pool([PS[:, i, :] for i in range(3)])
        misc = Pool([PS[:, i, :] for i in range(3, 8)])
        tmp = Pool(list(g_bufs))

        order = [(name, i) for name, n in UNITS for i in range(n)]
        n_sub = 2 * len(order)
        hi_tok, lo_tok, done = {}, {}, {}
        state = {"load": 0, "split": 0, "blk": 0}

        def load():
            u = state["load"]
            if u >= len(order):
                return
            state["load"] += 1
            name, i = order[u]
            waits = (lo_tok[2 * (u - NRAW) + 1],) if u >= NRAW else ()
            sp.dma(raw[:, u % NRAW, :], d[name][i], s_w[u % NRAW], *waits)

        def split():
            s = state["split"]
            if s >= n_sub:
                return
            state["split"] += 1
            u = s // 2
            src = raw[:, u % NRAW, (s % 2) * SUB:(s % 2 + 1) * SUB]
            landed = (s_w[u % NRAW], 16 * (u // NRAW + 1))
            used = (done[s - NW],) if s >= NW else ()
            b = s % NW
            hi_tok[s] = act(lambda e: e.activation(whi[:, b, :], src, ACT.Copy), landed, *used)
            lo_tok[s] = dve(lambda e: e.tensor_tensor(wlo[:, b, :], src, whi[:, b, :].bitcast(F32), ALU.subtract),
                            hi_tok[s], landed, *used)
            if s % 2:
                load()

        active, queue = [], []

        room = [2]

        def holding(n, task):
            return n, task

        def step(width=4):
            while queue and len(active) < width and queue[0][0] <= room[0]:
                n, g = queue.pop(0)
                room[0] -= n
                active.append((n, g))
            for n, g in list(active):
                try:
                    next(g)
                except StopIteration:
                    active.remove((n, g))
                    room[0] += n

        def pause(n):
            for _ in range(n):
                yield

        def drain():
            while queue or active:
                step()

        def mm(out_, l, r, start, stop, *waits, sig=False):
            return pe(lambda e: e.matmul(out_, l, r, start=start, stop=stop), *waits, sig=sig)

        def block(width, outs, pairs, first, last, waits):
            b = state["blk"]
            s, o = b // 8, (b % 8) * BLK
            state["blk"] = b + width
            ws = (hi_tok[s], lo_tok[s]) + tuple(waits)
            wh, wl = whi[:, s % NW, o:o + width * BLK], wlo[:, s % NW, o:o + width * BLK]
            end = (b + width) % 8 == 0
            tok = None
            for n, (out_, (xh, xl)) in enumerate(zip(outs, pairs)):
                ops = [(wh, xh), (wh, xl), (wl, xh)] if width == 1 else [(xh, wh), (xl, wh), (xh, wl)]
                for i, (l, r) in enumerate(ops):
                    sig = i == 2 and n == len(outs) - 1 and (end or last)
                    tok = mm(out_, l, r, first and i == 0, last and i == 2, *(ws if n == i == 0 else ()), sig=sig)
            if end:
                done[s] = tok
                split()
            if (b + width) % 4 == 0:
                step()
            return tok

        def mtiles(op, K, n=2, k0=0):
            bank, free = acc.get()
            for m in range(n):
                for k in range(K):
                    tok = block(1, [bank[:, m * T:(m + 1) * T]], [(op.hi(k0 + k), op.lo(k0 + k))], k == 0, k == K - 1,
                                op.tok[k0 + k] + (free if k == 0 else ()))
            return bank, tok

        def rows(op):
            (b0, f0), (b1, f1) = acc.get(), acc.get()
            for k in range(16):
                tok = block(2, [b0[:, 0:T], b1[:, 0:T]],
                            [(op.hi(k)[:, t * P:(t + 1) * P], op.lo(k)[:, t * P:(t + 1) * P]) for t in range(2)],
                            k == 0, k == 15, op.tok[k] + ((f0 + f1) if k == 0 else ()))
            return (b0, b1), tok

        def halves(op, k, n, src, *waits):
            hi, lo = op.hi(k, n), op.lo(k, n)
            a = act(lambda e: e.activation(hi, src, ACT.Copy), *waits, *op.free)
            b = dve(lambda e: e.tensor_tensor(lo, src, hi.bitcast(F32), ALU.subtract), a, *waits, *op.free)
            for i in range(n):
                op.tok[k + i] = (a, b)
            return b

        def root(dst, ms, scale, eps, *waits):
            a = act(lambda e: e.activation(dst, ms, ACT.Ln, bias=eps, scale=scale), *waits)
            return a, act(lambda e: e.activation(dst, dst, ACT.Exp, scale=-0.5), a)

        class Sum:

            def __init__(self):
                self.buf, self.w = tmp.get()
                self.tok = None

            def add(self, src, *waits):
                if self.tok is None:
                    self.tok = act(lambda e: e.activation(self.buf, src, ACT.Square), *waits, *self.w)
                    return self.tok
                q, w = tmp.get()
                a = act(lambda e: e.activation(q, src, ACT.Square), *waits, *w)
                self.tok = pool(lambda e: e.tensor_tensor(self.buf, self.buf, q, ALU.add), a, self.tok)
                tmp.put(q, self.tok)
                return a

        class Norm:

            def __init__(self, s, eps, r, cols=None, free=()):
                self.s, self.eps, self.r, self.cols, self.free, self.ok = s, eps, r, cols, free, None

            def task(self, lag=4):
                yield from pause(lag)
                s = self.s
                bank, f = misc.get()
                mm(bank[:, 0:T], ones, s.buf[:, 0:T], True, False, s.tok, *f)
                t = mm(bank[:, 0:T], ones, s.buf[:, T:2 * T], False, True, sig=True)
                if self.cols is not None:
                    for i in range(2):
                        mm(bank[:, T + i:T + i + 1], s.buf[:, i * P:(i + 1) * P], ones[:, 0:1], True, False)
                        t = mm(bank[:, T + i:T + i + 1], s.buf[:, T + i * P:T + (i + 1) * P], ones[:, 0:1], False, True,
                               sig=True)
                    root(self.cols, bank[:, T:T + 2], 1.0 / 2048, self.eps, t)
                a, self.ok = root(self.r, bank[:, 0:T], 1.0 / 2048, self.eps, t, *self.free)
                misc.put(bank, a)
                tmp.put(s.buf, t)

        def need(n):
            while n.ok is None:
                step()
            return n.ok

        def both(r):
            return r.unsqueeze(1).to_broadcast([P, 2, T])

        def two(x):
            return x.rearrange("p (a b) -> p a b", a=2)

        def times(dst, src, r, *waits):
            return dve(lambda e: e.tensor_tensor(two(dst), two(src), both(r), ALU.mult), *waits)

        def gained(op, k, src, gain, *waits):
            hi, lo, g = op.hi(k), op.lo(k), col(gain, k) if isinstance(gain, str) else gain[:, k:k + 1]
            a = act(lambda e: e.activation(hi, src, ACT.Copy, scale=g), *waits, *op.free)
            b = dve(lambda e: e.scalar_tensor_tensor(lo, src, g, hi.bitcast(F32), ALU.mult, ALU.subtract), a, *waits, *op.free)
            op.tok[k] = (a, b)

        act.dma(vec, d["vec"], s_v)
        for i in range(4):
            act.dma(xt(4 * i, 4), d["x"][:, 4 * i * T:(4 * i + 4) * T], s_x[i])
        act.dma(c1, d["c1"], s_c)
        for _ in range(NRAW):
            load()
        C_OK, V_OK = (s_c, 16), (s_v, 16)
        dve(None, V_OK, sig=False)
        act(None, V_OK, sig=False)
        split()
        for k in range(16):
            if k == 4:
                split()
            gained(H, k, xt(k), "norm_mix", (s_x[k // 4], 16))
        split()
        split()
        cr0 = dve(lambda e: e.tensor_copy(CR[:, 0:384], tri), C_OK)
        cr1 = dve(lambda e: e.tensor_copy(MNr, cst("mneg")))
        cr2 = dve(lambda e: e.tensor_copy(Ir, ident))
        RN, RSQ, RN2 = AR[:, 16896:17152], SM[:, 224:480], SM[:, 224:480]
        sx = Sum()
        nx = Norm(sx, col("eps5"), RN)

        def first_squares():
            for k in range(0, 16, 2):
                sx.add(xt(k, 2), (s_x[k // 4], 16))
                if k % 4:
                    yield
            pe(None, cr2, C_OK, sig=False)
            yield from nx.task(6)

        queue.append(holding(1, first_squares()))
        rsq = []

        mix = [AR[:, o:o + 512] for o in range(9728, G0, 512)]
        for b in mix:
            tmp.put(b)
        room[0] += 4
        Z, XS, CB = AR[:, 0:4096], AR[:, 4096:8192], AR[:, 8192:9728]

        def conv(dst, src, taps, bias, waits, width):
            w = [lambda i=i: taps(i) for i in range(width)]
            last = w[width - 1]()
            if bias is None:
                t = dve(lambda e: e.tensor_scalar(dst[:, 0:T], src[:, 0:T], last, None, ALU.mult), *waits)
            else:
                t = dve(lambda e: e.tensor_scalar(dst[:, 0:T], src[:, 0:T], last, bias, ALU.mult, ALU.add), *waits)
            for sh in range(1, width):
                wi = w[width - 1 - sh]()
                t = dve(lambda e, sh=sh, wi=wi: e.scalar_tensor_tensor(
                    dst[:, sh:T], src[:, 0:T - sh], wi, dst[:, sh:T], ALU.mult, ALU.add), t)
            return t

        def sc_norm(j, v, vt):
            q, w = tmp.get()
            a = act(lambda e: e.activation(q, v, ACT.Square), vt, *w)
            yield from pause(4)
            bank, f = misc.get()
            t = mm(bank, ones, q, True, True, a, *f, sig=True)
            a1, rt = root(q, bank, 1.0 / 128, col("eps5"), t)
            misc.put(bank, a1)
            for i in range(2):
                c = dve(lambda e, i=i: e.scalar_tensor_tensor(
                    v[:, i * T:(i + 1) * T], v[:, i * T:(i + 1) * T], col("sc_norm", 2 * j + i), q[:, i * T:(i + 1) * T],
                    ALU.mult, ALU.mult), rt, vt)
            tmp.put(q, c)
            tmp.put(v, halves(Y, 2 * j, 2, v, c))

        for j in range(8):
            bu, tu = mtiles(H, 16)
            u, w = tmp.get()
            bc, tc = mtiles(H, 16)
            if j == 0:
                rsq.append(dve(lambda e: e.tensor_tensor(RSQ, RN, RN, ALU.mult), need(nx)))
            a = times(u, bu, RSQ, tu, rsq[0], *w)
            acc.put(bu, a)
            c = dve(lambda e, u=u, bc=bc: e.tensor_tensor(u, bc, u, ALU.mult), tc, a)
            acc.put(bc, c)
            v, w = tmp.get()
            for i in range(2):
                vt = conv(v[:, i * T:(i + 1) * T], u[:, i * T:(i + 1) * T],
                          lambda n, i=i, j=j: col("sc_conv_w", n * 16 + 2 * j + i), None, (c,) + w, 3)
            tmp.put(u, vt)
            vt = times(v, v, RN, vt)
            bb, tb = mtiles(H, 16)
            vt = dve(lambda e, v=v, bb=bb: e.tensor_tensor(v, bb, v, ALU.mult), tb, vt)
            acc.put(bb, vt)
            queue.append(holding(1, sc_norm(j, v, vt)))

        def xbc(i0, dst, ready, *waits):
            bank, t = mtiles(H, 16)
            u, w = tmp.get()
            t = times(u, bank, RN, t, *w)
            acc.put(bank, t)
            q, w = tmp.get()
            for i in range(2):
                ct = conv(q[:, i * T:(i + 1) * T], u[:, i * T:(i + 1) * T],
                          lambda n, i=i: col("ssd_conv_w", n * 24 + i0 + i), col("ssd_conv_b", i0 + i), (t,) + w, 4)
            tmp.put(u, ct)
            a = act(lambda e: e.activation(dst if dst is not None else q, q, ACT.Silu), ct, *waits)
            if dst is not None:
                tmp.put(q, a)
            return q, a

        for i in range(4):
            _, bc_tok = xbc(16 + 2 * i, Z[:, i * 512:(i + 1) * 512], None)
        BM, CM_ = Z[:, 0:1024], Z[:, 1024:2048]
        cb_tok = [None] * 4

        def cb_task():
            yield from pause(4)
            for g in range(4):
                bank, f = misc.get()
                mm(bank[:, 0:256], BM[:, g * T:g * T + 128], CM_[:, g * T:(g + 1) * T], True, True, bc_tok, *f)
                t = mm(bank[:, 256:384], BM[:, g * T + 128:(g + 1) * T], CM_[:, g * T + 128:(g + 1) * T], True, True, sig=True)
                cb_tok[g] = act(lambda e, g=g, bank=bank: e.activation(CB[:, g * 384:(g + 1) * 384], bank[:, 0:384], ACT.Copy), t)
                misc.put(bank, cb_tok[g])
                yield

        queue.append(holding(0, cb_task()))
        bdt, tdt = mtiles(H, 16, 1)
        dtT = SM[:, 0:64]
        nacs = SM[:, 64:128]
        arow = SM[:, 128:160]
        adt = SM[:, 160:224]
        ssd_ready = []

        def dt_task():
            x, w = tmp.get()
            y, w2 = tmp.get()
            xv, ab, e1, u1 = (q[0:32, :] for q in (x[:, 0:T], x[:, T:2 * T], y[:, 0:T], y[:, T:2 * T]))
            c = dve(lambda e: e.tensor_tensor(xv, bdt[0:32, 0:T], RN[0:32, :], ALU.mult), tdt, *w, *w2)
            acc.put(bdt, c)
            c = dve(lambda e: e.tensor_scalar(xv, xv, col("dt_bias")[0:32, :], None, ALU.add), c)
            a = act(lambda e: e.activation(ab, xv, ACT.Abs), c)
            a = act(lambda e: e.activation(e1, ab, ACT.Exp, scale=-1.0), a)
            c1_ = dve(lambda e: e.tensor_scalar(u1, e1, 1.0, None, ALU.add), a)
            a = act(lambda e: e.activation(ab, u1, ACT.Ln), c1_)
            yield from pause(2)
            c = dve(lambda e: e.tensor_scalar(u1, u1, -1.0, None, ALU.add), a)
            m, wm = tmp.get()
            mk, rc = m[0:32, 0:T], m[0:32, T:2 * T]
            c = dve(lambda e: e.tensor_scalar(mk, u1, 0.0, None, ALU.is_equal), c, *wm)
            k1 = dve(lambda e: e.tensor_tensor(u1, u1, mk, ALU.add), c)
            k2 = dve(lambda e: e.tensor_tensor(ab, ab, mk, ALU.add), c)
            k3 = dve(lambda e: e.reciprocal(rc, u1), k1)
            k4 = dve(lambda e: e.tensor_tensor(ab, ab, e1, ALU.mult), k2)
            k5 = dve(lambda e: e.tensor_tensor(ab, ab, rc, ALU.mult), k3, k4)
            k6 = dve(lambda e: e.scalar_tensor_tensor(xv, xv, 0.0, ab, ALU.max, ALU.add), k5)
            yield from pause(4)
            bank, f = misc.get()
            for t in range(2):
                tt = pe(lambda e, t=t: e.transpose(bank[:, t * 32:(t + 1) * 32], xv[:, t * P:(t + 1) * P], ident[0:32, 0:32]),
                        k6, *f)
            c = dve(lambda e: e.tensor_copy(dtT, bank[:, 0:64]), tt)
            misc.put(bank, c)
            tmp.put(x, tt)
            tmp.put(y, k6)
            tmp.put(m, k6)
            ar = act(lambda e: e.activation(arow, vec[:, VOFF["a_log"][0]:VOFF["a_log"][0] + 32], ACT.Exp))
            for t in range(2):
                c2 = dve(lambda e, t=t: e.scalar_tensor_tensor(adt[:, t * 32:(t + 1) * 32], dtT[:, t * 32:(t + 1) * 32], -1.0,
                                                                 arow, ALU.mult, ALU.mult), c, ar)
            h = dve(lambda e: e.tensor_copy(ADT[:, 0:2, :], adt), c2)
            l = dve(lambda e: e.tensor_tensor(ADT[:, 2:4, :], adt, ADT[:, 0:2, :].bitcast(F32).rearrange("p a b -> p (a b)"),
                                              ALU.subtract), h)
            yield from pause(3)
            bank, f = misc.get()
            mm(bank[:, 0:32], tri[:, 0:128], adt[:, 0:32], True, True, c2, *f)
            mm(bank[:, 32:64], ones, adt[:, 0:32], True, False)
            t = mm(bank[:, 32:64], tri[:, 0:128], adt[:, 32:64], False, True, sig=True)
            c = dve(lambda e: e.tensor_scalar(nacs, bank[:, 0:64], -1.0, None, ALU.mult), t)
            misc.put(bank, c)
            ssd_ready.extend([c, l])

        queue.append(holding(3, dt_task()))
        xs_tok = [None] * 8

        def xs_task(j, q, a):
            yield from pause(5)
            bank, f = misc.get()
            for t in range(2):
                for i in range(2):
                    tt = pe(lambda e, t=t, i=i: e.transpose(bank[:, t * T + i * P:t * T + (i + 1) * P],
                                                              q[:, i * T + t * P:i * T + (t + 1) * P], ident), a, *f)
            dst = XS.rearrange("p (t n) -> p t n", t=2)[:, :, j * T:(j + 1) * T]
            xs_tok[j] = act(lambda e: e.activation(dst, bank.rearrange("p (t n) -> p t n", t=2), ACT.Copy), tt)
            misc.put(bank, xs_tok[j])
            tmp.put(q, tt)

        for j in range(8):
            q, a = xbc(2 * j, None, None)
            queue.append(holding(0, xs_task(j, q, a)))
        while None in cb_tok:
            step()
        z_tok = [None] * 16
        def ssd_pair(i):
            while len(ssd_ready) < 2 or xs_tok[i // 2] is None:
                yield
            es = []
            for h in (2 * i, 2 * i + 1):
                g = h // 8
                bank, f = misc.get()
                w0 = [ADT[:, 2 * p, h:h + 1].to_broadcast([P, P]) for p in range(2)]
                w1 = [ADT[:, 2 * p + 1, h:h + 1].to_broadcast([P, P]) for p in range(2)]
                mm(bank[:, 0:384], w0[0], TRIr, True, False, *ssd_ready, *f)
                mm(bank[:, 0:384], w0[1], TRIr, False, False)
                for p in range(2):
                    for o in (128, 256):
                        mm(bank[:, o:o + 128], w1[p], TRIr[:, 0:128], False, False)
                mm(bank[:, 0:128], Ir, MNr, False, False)
                t = mm(bank[:, 256:384], Ir, MNr, False, True, sig=True)
                E, w = tmp.get()
                a0 = act(lambda e, h=h, E=E, bank=bank: e.activation(E[:, 0:256], bank[:, 0:256], ACT.Exp,
                                                                       bias=nacs[:, h:h + 1]), t, *w, *ssd_ready)
                a1 = act(lambda e, h=h, E=E, bank=bank: e.activation(E[:, 256:384], bank[:, 256:384], ACT.Exp,
                                                                       bias=nacs[:, 32 + h:33 + h]))
                misc.put(bank, a1)
                cb = CB[:, g * 384:(g + 1) * 384]
                c0 = dve(lambda e, h=h, E=E, cb=cb: e.scalar_tensor_tensor(
                    E[:, 0:256], cb[:, 0:256], dtT[:, h:h + 1], E[:, 0:256], ALU.mult, ALU.mult), a0, cb_tok[g])
                c1_ = dve(lambda e, h=h, E=E, cb=cb: e.scalar_tensor_tensor(
                    E[:, 256:384], cb[:, 256:384], dtT[:, 32 + h:33 + h], E[:, 256:384], ALU.mult, ALU.mult), a1)
                for o, cc in ((0, c0), (256, c1_)):
                    c = dve(lambda e, h=h, E=E, o=o: e.scalar_tensor_tensor(
                        E[:, o:o + 128], ident, col("d_skip", h), E[:, o:o + 128], ALU.mult, ALU.add), cc)
                es.append((h, E, c))
            yield from pause(6)
            while z_tok[i] is None:
                yield
            bank, f = misc.get()
            for h, E, c in es:
                o = bank[64 * (h % 2):64 * (h % 2) + 64, 0:T]
                mm(o, XS[:, 64 * h:64 * h + 64], E[:, 0:256], True, False, c, xs_tok[h // 4], *f)
                t = mm(o[:, 128:256], XS[:, 2048 + 64 * h:2048 + 64 * h + 64], E[:, 256:384], False, True, sig=True)
                tmp.put(E, t)
            zt = Z[:, i * T:(i + 1) * T]
            z_tok[i] = dve(lambda e: e.tensor_tensor(zt, bank[:, 0:T], zt, ALU.mult), t, z_tok[i])
            misc.put(bank, z_tok[i])
            pair_done[i] = True

        def ssd_group(g):
            while not all(pair_done[4 * g:4 * g + 4]) or not z_all:
                yield
            zs = [Z[:, (4 * g + 2 * p) * T:(4 * g + 2 * p + 2) * T] for p in range(2)]
            qs = []
            for p in range(2):
                q, w = tmp.get()
                a = act(lambda e, p=p, q=q: e.activation(q, zs[p], ACT.Square), z_tok[4 * g + 2 * p], z_tok[4 * g + 2 * p + 1], *w)
                qs.append(q)
            yield from pause(4)
            bank, f = misc.get()
            for n in range(4):
                t = mm(bank[:, 0:T], ones, qs[n // 2][:, (n % 2) * T:(n % 2 + 1) * T], n == 0, n == 3, a, *f, sig=n == 3)
            r = qs[0][:, 0:T]
            a1, rt = root(r, bank[:, 0:T], 1.0 / 512, col("eps5"), t)
            misc.put(bank, a1)
            tmp.put(qs[1], t)
            yield from pause(2)
            for p in range(2):
                for i in range(2):
                    k = 4 * g + 2 * p + i
                    c = dve(lambda e, k=k: e.scalar_tensor_tensor(
                        Z[:, k * T:(k + 1) * T], Z[:, k * T:(k + 1) * T], col("ssd_norm", k), r, ALU.mult, ALU.mult),
                        rt, z_tok[k])
                last = halves(H, 4 * g + 2 * p, 2, zs[p], c)
            tmp.put(qs[0], c)
            z_end.append(last)

        pair_done, z_all, z_end = [False] * 16, [], []
        for g in range(4):
            for i in range(4):
                queue.append(holding(2, ssd_pair(4 * g + i)))
            queue.append(holding(2, ssd_group(g)))
        for j in range(8):
            bank, t = mtiles(H, 16)
            zj = Z[:, j * 512:(j + 1) * 512]
            c = times(zj, bank, RN, t, *cb_tok)
            acc.put(bank, c)
            a = act(lambda e, zj=zj: e.activation(zj, zj, ACT.Silu), c)
            z_tok[2 * j] = z_tok[2 * j + 1] = a
        H.free = (t,)

        z_all.append(t)

        def residual(bank, t, j, s=None, op=None, gain=None):
            c = dve(lambda e: e.tensor_tensor(xt(2 * j, 2), xt(2 * j, 2), bank, ALU.add), t)
            acc.put(bank, c)
            if op is not None:
                for i in range(2):
                    gained(op, 2 * j + i, xt(2 * j + i), gain, c)
            if s is not None:
                s.add(xt(2 * j, 2), c)

        for j in range(8):
            bank, t = mtiles(Y, 16)
            residual(bank, t, j)
        Y.free = (t,)
        drain()

        act.dma(XS, d["mem"], s_m, t, *[z_tok[i] for i in range(16)])

        mcol = SM[:, 200:202]
        sm = Sum()
        rmb, rmw = tmp.get()
        nm = Norm(sm, col("eps5"), rmb[:, 0:T], mcol, rmw)

        def mem_squares():
            for k in range(0, 16, 2):
                sm.add(XS[:, k * T:(k + 2) * T], (s_m, 16))
                if k % 4:
                    yield
            yield from nm.task()

        def mem_operand():
            for k in range(16):
                gained(H, k, XS[:, k * T:(k + 1) * T], "mem_norm", (s_m, 16))
                if k % 2:
                    yield

        queue.append(holding(1, mem_squares()))
        sx = Sum()
        for j in range(8):
            bank, t = mtiles(H, 16)
            residual(bank, t, j, sx, Y, "norm_xa")
        H.free = (t,)
        drain()

        nx = Norm(sx, col("eps5"), RN)
        queue.append(holding(0, nx.task()))
        queue.append(holding(0, mem_operand()))
        KT, VM, QT = Z[:, 0:1024], Z[:, 1024:2048], Z[:, 2048:3072]
        for j in range(2):
            bank, t = mtiles(Y, 16)
            dst = QT[:, j * 512:(j + 1) * 512]
            q_tok = dve(lambda e, bank=bank, dst=dst: e.scalar_tensor_tensor(
                two(dst), two(bank), 128.0 ** -0.5, both(RN), ALU.mult, ALU.mult), t, need(nx), *z_end)
            acc.put(bank, q_tok)
        Y.free = (t,)
        drain()
        for j in range(2):
            bank, t = mtiles(H, 16)
            k_tok = times(KT[:, j * 512:(j + 1) * 512], bank, rmb[:, 0:T], t, nm.ok, *z_end)
            acc.put(bank, k_tok)
        tmp.put(rmb, k_tok)
        v_tok = []
        stat = SM[:, 160:192]

        def xa_head(h):
            st = stat[:, 8 * h:8 * h + 8]
            bank, f = misc.get()
            for t in range(2):
                tt = mm(bank[:, t * T:(t + 1) * T], QT[:, h * T + t * P:h * T + (t + 1) * P], KT[:, h * T:(h + 1) * T],
                        True, True, q_tok, k_tok, *f, sig=t == 1)
            c = dve(lambda e: e.tensor_reduce(st[:, 0:2], bank.rearrange("p (t n) -> p t n", t=2), AX, ALU.max, negate=True), tt)
            Pb, w = tmp.get()
            for t in range(2):
                a = act(lambda e, t=t: e.activation(Pb[:, t * T:(t + 1) * T], bank[:, t * T:(t + 1) * T], ACT.Exp,
                                                     bias=st[:, t:t + 1], accum_out=st[:, 2 + t:3 + t]), c, *w)
            misc.put(bank, a)
            c = dve(lambda e: e.reciprocal(st[:, 4:6], st[:, 2:4]), a)
            for t in range(2):
                cn = dve(lambda e, t=t: e.tensor_scalar(Pb[:, t * T:(t + 1) * T], Pb[:, t * T:(t + 1) * T],
                                                        st[:, 4 + t:5 + t], None, ALU.mult), c)
            yield from pause(5)
            bank, f = misc.get()
            for m in range(2):
                for t in range(2):
                    tt = pe(lambda e, m=m, t=t: e.transpose(bank[:, m * T + t * P:m * T + (t + 1) * P],
                                                              Pb[:, t * T + m * P:t * T + (m + 1) * P], ident), cn, *f)
            PT, w = tmp.get()
            a = act(lambda e: e.activation(PT, bank, ACT.Copy), tt, *w)
            misc.put(bank, a)
            tmp.put(Pb, tt)
            yield from pause(2)
            while len(v_tok) < 4:
                yield
            bank, f = misc.get()
            for m in range(2):
                tt = mm(bank[:, 0:T], VM[:, m * 512 + h * P:m * 512 + (h + 1) * P], PT[:, m * T:(m + 1) * T],
                        m == 0, m == 1, a, *v_tok, *f, sig=m == 1)
            tmp.put(PT, tt)
            misc.put(bank, halves(Y, h, 1, bank[:, 0:T], tt))

        for h in range(4):
            queue.append(holding(2, xa_head(h)))
        for j in range(2):
            banks, t = rows(H)
            for m in range(2):
                v_tok.append(act(lambda e, j=j, m=m, b=banks[m]: e.activation(
                    VM[:, m * 512 + j * T:m * 512 + (j + 1) * T], b[:, 0:T], ACT.Copy, scale=mcol[:, m:m + 1]), t, nm.ok))
                acc.put(banks[m], v_tok[-1])
        H.free = (t,)
        drain()
        c2_free = [t for b, toks in tmp.free if any(b is m for m in mix) for t in toks]
        tmp.free = [x for x in tmp.free if not any(x[0] is m for m in mix)]
        room[0] -= 5
        sx = Sum()
        for j in range(8):
            bank, t = mtiles(Y, 4)
            residual(bank, t, j, sx, H, "norm_ffn")
        Y.free = (t,)

        def ffn(conv2, eps, op, gain):
            s = None
            n = Norm(sx, eps, RN)
            queue.append(holding(0, n.task(5)))
            for a0, a1 in PARTS:
                for j in range(a0, a1, 2):
                    bg, tg = mtiles(H, 16)
                    q, w = tmp.get()
                    tg = times(q, bg, RN, tg, need(n), *w)
                    acc.put(bg, tg)
                    if conv2:
                        u, w = tmp.get()
                        for i in range(2):
                            c = conv(u[:, i * T:(i + 1) * T], q[:, i * T:(i + 1) * T],
                                     lambda m, i=i, j=j: col("conv_w_2", m * 44 + j + i), col("conv_b_2", j + i), (tg,) + w, 3)
                        tmp.put(q, c)
                        q, tg = u, c
                    a = act(lambda e, q=q: e.activation(q, q, ACT.Silu), tg)
                    a = times(q, q, RN, a)
                    bu, tu = mtiles(H, 16)
                    c = dve(lambda e, q=q, bu=bu: e.tensor_tensor(q, bu, q, ALU.mult), tu, a)
                    acc.put(bu, c)
                    tmp.put(q, halves(Y, j - a0, 2, q, c))
                if a1 == 44:
                    H.free = (tu,)
                    s = Sum()
                for j in range(8):
                    bank, t = mtiles(Y, a1 - a0)
                    residual(bank, t, j, s, op if s is not None else None, gain)
                Y.free = (t,)
            return s

        g12 = SM[:, 480:496]
        g12_tok = dve(lambda e: e.tensor_tensor(g12, vec[:, VOFF["norm_final"][0]:VOFF["norm_final"][0] + 16],
                                                vec[:, VOFF["attn_norm_2"][0]:VOFF["attn_norm_2"][0] + 16], ALU.mult))
        act(None, g12_tok, sig=False)
        dve(None, g12_tok, sig=False)
        sx = ffn(False, col("eps5"), H, g12)

        c2 = AR[:, 9216:9216 + NC2]
        act.dma(c2, d["c2"], s_c2, *c2_free)

        def k2(name):
            o, w = C2OFF[name]
            return c2[:, o:o + w]

        n1 = Norm(sx, col("eps5"), RN, SM[:, 496:498])
        s2 = Sum()
        n2 = Norm(s2, col("eps6"), RN2, SM[:, 498:500])
        rr = []

        def middle():
            yield from n1.task()
            for k in range(16):
                c = dve(lambda e, k=k: e.scalar_tensor_tensor(xt(k), xt(k), col("norm_final", k), RN, ALU.mult, ALU.mult),
                        n1.ok, *H.tok[k])
                if k % 2:
                    s2.add(xt(k - 1, 2), c)
                if k % 4 == 3:
                    yield
            yield from n2.task(5)
            c = dve(lambda e: e.tensor_tensor(RN, RN, RN2, ALU.mult), n2.ok, c)
            rr.append(dve(lambda e: e.tensor_tensor(SM[:, 496:498], SM[:, 496:498], SM[:, 498:500], ALU.mult), c))

        queue.append(holding(1, middle()))
        C2_OK = (s_c2, 16)
        pe(None, C2_OK, sig=False)
        dve(None, C2_OK, sig=False)

        lam = SM[:, 0:16]
        lv = k2("lam")
        Dr, MCr = CR[:, 0:384], CR[:, 384:448]
        dr_tok = dve(lambda e: e.tensor_copy(Dr, k2("dist")))
        mc_tok = dve(lambda e: e.tensor_copy(MCr, k2("mc")))
        q, w = tmp.get()
        for i in range(2):
            c = dve(lambda e, i=i, q=q: e.tensor_tensor(q[:, 64 * i:64 * i + 64], lv[:, 128 * i:128 * i + 64],
                                                        lv[:, 128 * i + 64:128 * i + 128], ALU.mult), *w)
        c = dve(lambda e: e.tensor_reduce(lam[:, 0:2], q[:, 0:128].rearrange("p (a b) -> p a b", a=2), AX, ALU.add), c)
        tmp.put(q, c)
        a = act(lambda e: e.activation(lam[:, 2:4], lam[:, 0:2], ACT.Exp), c)
        c = dve(lambda e: e.tensor_tensor(lam[:, 4:5], lam[:, 2:3], lam[:, 3:4], ALU.subtract), a)
        c = dve(lambda e: e.tensor_scalar(lam[:, 4:5], lam[:, 4:5], 0.8 - 0.6, None, ALU.add), c)
        c = dve(lambda e: e.tensor_scalar(lam[:, 5:6], lam[:, 4:5], -1.0, None, ALU.mult), c)
        c = dve(lambda e: e.tensor_tensor(lam[:, 6:7], lam[:, 4:5], lam[:, 5:6], ALU.max), c)
        c = dve(lambda e: e.tensor_scalar(lam[:, 6:7], lam[:, 6:7], 1.0, None, ALU.max), c)
        c = dve(lambda e: e.reciprocal(lam[:, 7:8], lam[:, 6:7]), c)
        c0 = dve(lambda e: e.tensor_tensor(lam[:, 8:9], lam[:, 5:6], lam[:, 7:8], ALU.mult), c)
        c1_ = dve(lambda e: e.tensor_tensor(lam[:, 9:10], lam[:, 7:8], lam[:, 7:8], ALU.mult), c)
        c1_ = dve(lambda e: e.tensor_scalar(lam[:, 9:10], lam[:, 9:10], 1e-5, None, ALU.mult), c1_)
        c2_ = dve(lambda e: e.tensor_scalar(lam[:, 10:11], col("diff_subln_2"), 1.0 - (0.8 - 0.6), None, ALU.mult))
        lam_ok = (c0, c1_, c2_)
        for i in range(3):
            o = 9216 + C2_KEPT + 512 * i
            tmp.put(AR[:, o:o + 512], dr_tok, mc_tok, lam_ok[1])
        room[0] += 5
        inv, nlam, eps_a, gain_a = lam[:, 7:8], lam[:, 8:9], lam[:, 9:10], lam[:, 10:11]

        base = 9216
        G_row, gw = tmp.get()
        g8 = G_row[0:8, :]
        act.dma(g8[:, 127:319], d["rel"], s_g, *gw)
        c = dve(lambda e: e.tensor_copy(g8[:, 0:127], g8[:, 127:128].to_broadcast([8, 127])), (s_g, 16), *gw)
        c = dve(lambda e: e.tensor_copy(g8[:, 319:511], g8[:, 318:319].to_broadcast([8, 192])))
        c = dve(lambda e: e.tensor_copy(g8[:, 511:512], g8[:, 318:319]))
        scratch = nc.dram_tensor("rel_rows", [8, 512], F32).ap()
        act.dma(scratch, g8, s_g, c)
        hank_src = bass.AP(tensor=scratch.tensor, offset=0, ap=[[1, P], [512, 8], [1, 256]])
        tmp.put(G_row, (s_g, 32))

        QA, KA, VA = AR[:, 0:2048], AR[:, 2048:4096], AR[:, 4096:6144]
        QB, KB, VB = AR[:, 6144:7168], AR[:, 7168:8192], AR[:, 8192:9216]
        QC, KC, VC = AR[:, 0:1024], AR[:, 1024:2048], AR[:, 2048:3072]
        HK = AR[:, 3072:5120]

        def qk(dq, dk, n, *waits):
            todo = [(dst, sc, j) for dst, sc in ((dq, 0.125), (dk, 1.0)) for j in range(n // 2)]
            late = 0 if rr else 2
            banks = []
            for i, (dst, sc, j) in enumerate(todo):
                banks.append(mtiles(H, 16))
                if i < late:
                    continue
                while not rr:
                    step()
                for dst, sc, j in todo[0:i + 1] if i == late else [todo[i]]:
                    bank, t = banks.pop(0)
                    b_ = dve(lambda e, j=j, bank=bank, dst=dst, sc=sc: e.scalar_tensor_tensor(
                        two(dst[:, j * 512:(j + 1) * 512]), two(bank), sc, both(RN), ALU.mult, ALU.mult), t, rr[0], *waits)
                    acc.put(bank, b_)
            return b_, t

        def values(dv, n, *waits):
            for j in range(n // 2):
                banks, t = rows(H)
                for m in range(2):
                    a = act(lambda e, j=j, m=m, b=banks[m]: e.activation(
                        dv[:, m * n * P + j * T:m * n * P + (j + 1) * T], b[:, 0:T], ACT.Copy,
                        scale=SM[:, 496 + m:497 + m]), t, rr[0], *waits)
                    acc.put(banks[m], a)
            return a, t

        a_tok, t = qk(QA, KA, 8)

        def scaled(o_bank, tt, mat, scale, eps, gain, tile, *waits):
            q, w = tmp.get()
            a = act(lambda e: e.activation(q[:, 0:T], o_bank[:, 0:T], ACT.Square), tt, *w, *waits)
            yield from pause(2)
            bank, f = misc.get()
            t = mm(bank[:, 0:T], mat, q[:, 0:T], True, True, a, *f, sig=True)
            a1, rt = root(q[:, T:2 * T], bank[:, 0:T], scale, eps, t)
            misc.put(bank, a1)
            yield
            c = dve(lambda e: e.scalar_tensor_tensor(q[:, 0:T], o_bank[:, 0:T], gain, q[:, T:2 * T], ALU.mult, ALU.mult), rt)
            misc.put(o_bank, c)
            tmp.put(q, halves(Y, tile, 1, q[:, 0:T], c))

        def turn(Wb, wt):
            bank, f = misc.get()
            for o, s in ((0, 0), (128, 128), (256, 256)):
                tt = pe(lambda e, o=o, s=s: e.transpose(bank[:, o:o + 128], Wb[:, s:s + 128], ident), wt, *f)
            WT, w = tmp.get()
            a = act(lambda e: e.activation(WT[:, 0:384], bank[:, 0:384], ACT.Copy), tt, *w)
            misc.put(bank, a)
            tmp.put(Wb, tt)
            return WT, a

        def diff_head(h):
            st = SM[:, 16 + 16 * h:32 + 16 * h]
            si = dve(lambda e: e.tensor_scalar(sI[h % 2], ident, 2.0 ** -(h + 1), None, ALU.mult), *si_free[h % 2])
            Ps = []
            for c in range(2):
                bank, f = misc.get()
                lo_, hi_ = 64 * c, 64 * c + 64
                mm(bank[:, 0:384], sI[h % 2], Dr, True, False, si, dr_tok, *f)
                mm(bank[:, 0:128], QA[lo_:hi_, h * T:h * T + 128], KA[lo_:hi_, h * T:h * T + 128], False, False, a_tok)
                tt = mm(bank[:, 128:384], QA[lo_:hi_, h * T + 128:(h + 1) * T], KA[lo_:hi_, h * T:(h + 1) * T],
                        False, True, sig=True)
                for o, n, i in ((0, 128, 0), (128, 256, 1)):
                    cm = dve(lambda e, o=o, n=n, i=i, bank=bank, c=c: e.tensor_reduce(
                        st[:, 2 * c + i:2 * c + i + 1], bank[:, o:o + n], AX, ALU.max, negate=True), tt)
                Pb, w = tmp.get()
                for o, n, i in ((0, 128, 0), (128, 256, 1)):
                    a = act(lambda e, o=o, n=n, i=i, bank=bank, c=c, Pb=Pb: e.activation(
                        Pb[:, o:o + n], bank[:, o:o + n], ACT.Exp, bias=st[:, 2 * c + i:2 * c + i + 1],
                        accum_out=st[:, 4 + 2 * c + i:5 + 2 * c + i]), cm, *w)
                misc.put(bank, a)
                Ps.append(Pb)
            si_free[h % 2] = (tt,)
            r = dve(lambda e: e.reciprocal(st[:, 8:12], st[:, 4:8]), a)
            r0 = dve(lambda e: e.tensor_scalar(st[:, 8:10], st[:, 8:10], inv, None, ALU.mult), r, *lam_ok)
            r1 = dve(lambda e: e.tensor_scalar(st[:, 10:12], st[:, 10:12], nlam, None, ALU.mult), r)
            for o, n, i in ((0, 128, 0), (128, 256, 1)):
                m = dve(lambda e, o=o, n=n, i=i: e.tensor_scalar(Ps[1][:, o:o + n], Ps[1][:, o:o + n],
                                                                 st[:, 10 + i:11 + i], None, ALU.mult), r1)
                wt = dve(lambda e, o=o, n=n, i=i: e.scalar_tensor_tensor(
                    Ps[0][:, o:o + n], Ps[0][:, o:o + n], st[:, 8 + i:9 + i], Ps[1][:, o:o + n], ALU.mult, ALU.add), m, r0)
            tmp.put(Ps[1], wt)
            yield from pause(7)
            WT, a = turn(Ps[0], wt)
            yield from pause(2)
            while not av_tok:
                yield
            bank, f = misc.get()
            mm(bank[:, 0:T], VA[:, h * P:(h + 1) * P], WT[:, 0:256], True, False, a, av_tok[0], *f)
            tt = mm(bank[:, 128:256], VA[:, 1024 + h * P:1024 + (h + 1) * P], WT[:, 256:384], False, True, sig=True)
            tmp.put(WT, tt)
            pv_tok.append(tt)
            yield from scaled(bank, tt, ones, 1.0 / 128, eps_a, gain_a, h, *lam_ok)

        si_free = [(cr2,), (cr2,)]
        pv_tok = []
        for h in range(8):
            queue.append(holding(2, diff_head(h)))
        av_tok = []
        av_tok.append(values(VA, 8)[0])
        b_tok, t = qk(QB, KB, 4)
        bv_tok, t = values(VB, 4)
        drain()
        hk = [*pv_tok, (s_g, 32)]
        act.dma(HK.rearrange("p (h n) -> p h n", h=8), hank_src, s_h, *hk)
        NM, CMk, TRI2, BD, J = k2("nm"), k2("cm"), k2("tri2"), k2("bd"), k2("flip")

        def stick_pair(i):
            o_bank = None
            for h in (2 * i, 2 * i + 1):
                lo_, hi_ = 64 * (h % 2), 64 * (h % 2) + 64
                bank, f = misc.get()
                mm(bank[:, 0:256], KB[lo_:hi_, i * T:i * T + 128], QB[lo_:hi_, i * T:(i + 1) * T], True, True, b_tok, *f)
                tt = mm(bank[:, 256:384], KB[lo_:hi_, i * T + 128:(i + 1) * T], QB[lo_:hi_, i * T + 128:(i + 1) * T],
                        True, True, sig=True)
                z, w = tmp.get()
                q, w2 = tmp.get()
                z_, q_ = z[:, 0:384], q[:, 0:384]
                zc = dve(lambda e, bank=bank, z_=z_: e.tensor_tensor(z_, bank[:, 0:384], CMk, ALU.mult), tt, *w)
                misc.put(bank, zc)
                a = act(lambda e, z_=z_, q_=q_: e.activation(q_, z_, ACT.Abs), zc, *w2)
                a = act(lambda e, q_=q_: e.activation(q_, q_, ACT.Exp, scale=-1.0), a)
                a = act(lambda e, q_=q_: e.activation(q_, q_, ACT.Ln, bias=1.0), a)
                c = dve(lambda e, z_=z_, q_=q_: e.scalar_tensor_tensor(q_, z_, 0.0, q_, ALU.max, ALU.add), a)
                c = dve(lambda e, q_=q_: e.tensor_tensor(q_, q_, NM, ALU.mult), c)
                yield from pause(4)
                bank, f = misc.get()
                mm(bank[:, 0:256], TRI2, q[:, 0:256], True, False, c, *f)
                mm(bank[:, 128:256], ones, q[:, 256:384], False, True)
                tt = mm(bank[:, 256:384], TRI2, q[:, 256:384], True, True, sig=True)
                tmp.put(q, tt)
                c = dve(lambda e, bank=bank, z_=z_: e.tensor_tensor(z_, bank[:, 0:384], z_, ALU.add), tt)
                misc.put(bank, c)
                a = act(lambda e, z_=z_: e.activation(z_, z_, ACT.Exp), c)
                c = dve(lambda e, z_=z_: e.tensor_tensor(z_, z_, CMk, ALU.mult), a)
                yield from pause(3)
                if o_bank is None:
                    o_bank, f = misc.get()
                else:
                    f = ()
                o = o_bank[lo_:hi_, 0:T]
                mm(o, VB[:, h * 64:h * 64 + 64], z[:, 0:256], True, False, c, bv_tok, *f)
                tt = mm(o[:, 128:256], VB[:, 512 + h * 64:512 + h * 64 + 64], z[:, 256:384], False, True, sig=True)
                tmp.put(z, tt)
            yield from scaled(o_bank, tt, BD, 1.0 / 64, col("eps6"), col("sb_norm_2", i), 8 + i)

        def band_pair(i):
            o_bank = None
            for h in (2 * i, 2 * i + 1):
                lo_, hi_ = 64 * (h % 2), 64 * (h % 2) + 64
                st = SM[:, 96 + 16 * h:112 + 16 * h]
                bank, f = misc.get()
                hk_ = HK[:, h * T:(h + 1) * T]
                mm(bank[:, 0:128], J, hk_[:, 128:256], True, False, (s_h, 16), *f)
                mm(bank[:, 0:128], QC[lo_:hi_, i * T:i * T + 128], KC[lo_:hi_, i * T:i * T + 128], False, False, c_tok)
                mm(bank[:, 64:128], Ir, MCr, False, True, mc_tok)
                mm(bank[:, 128:384], J, hk_, True, False)
                mm(bank[:, 128:384], QC[lo_:hi_, i * T + 128:(i + 1) * T], KC[lo_:hi_, i * T:(i + 1) * T], False, False)
                tt = mm(bank[:, 320:384], Ir, MCr, False, True, sig=True)
                for o, n, k in ((0, 128, 0), (128, 256, 1)):
                    cm = dve(lambda e, o=o, n=n, k=k, bank=bank, st=st: e.tensor_reduce(
                        st[:, k:k + 1], bank[:, o:o + n], AX, ALU.max, negate=True), tt)
                Pb, w = tmp.get()
                for o, n, k in ((0, 128, 0), (128, 256, 1)):
                    a = act(lambda e, o=o, n=n, k=k, bank=bank, Pb=Pb, st=st: e.activation(
                        Pb[:, o:o + n], bank[:, o:o + n], ACT.Exp, bias=st[:, k:k + 1], accum_out=st[:, 2 + k:3 + k]), cm, *w)
                misc.put(bank, a)
                r = dve(lambda e, st=st: e.reciprocal(st[:, 4:6], st[:, 2:4]), a)
                for o, n, k in ((0, 128, 0), (128, 256, 1)):
                    wt = dve(lambda e, o=o, n=n, k=k, Pb=Pb, st=st: e.tensor_scalar(
                        Pb[:, o:o + n], Pb[:, o:o + n], st[:, 4 + k:5 + k], None, ALU.mult), r)
                yield from pause(5)
                WT, a = turn(Pb, wt)
                yield from pause(2)
                if o_bank is None:
                    o_bank, f = misc.get()
                else:
                    f = ()
                o = o_bank[lo_:hi_, 0:T]
                mm(o, VC[:, h * 64:h * 64 + 64], WT[:, 0:256], True, False, a, cv_tok, *f)
                tt = mm(o[:, 128:256], VC[:, 512 + h * 64:512 + h * 64 + 64], WT[:, 256:384], False, True, sig=True)
                tmp.put(WT, tt)
            yield from scaled(o_bank, tt, BD, 1.0 / 64, col("eps6"), col("ch_norm_2", i), 12 + i)

        for i in range(4):
            queue.append(holding(2, stick_pair(i)))
        c_tok, t = qk(QC, KC, 4, *pv_tok)
        cv_tok, t = values(VC, 4, *pv_tok)
        H.free = (t,)
        for i in range(4):
            queue.append(holding(2, band_pair(i)))
        for j in range(8):
            bank, t = mtiles(Y, 8)
            residual(bank, t, j)
        drain()
        sx = Sum()
        for j in range(8):
            bank, t = mtiles(Y, 8, 2, 8)
            residual(bank, t, j, sx, H, "ffn_norm_2")
        Y.free = (t,)
        sx = ffn(True, col("eps6"), None, None)
        outs = 0
        nx = Norm(sx, col("eps6"), RN)
        for _ in nx.task():
            pass
        for k in range(16):
            c = dve(lambda e, k=k: e.scalar_tensor_tensor(xt(k), xt(k), col("final_norm_2", k), RN, ALU.mult, ALU.mult), nx.ok)
            if k % 4 == 3:
                sp.dma(out[:, (k - 3) * T:(k + 1) * T], xt(k - 3, 4), s_out, c)
                outs += 16
        sp(None, (s_out, outs), (s_g, 32), (s_h, 16), sig=False)
        assert state["blk"] == 16 * len(order), (state, len(order))

        with nc.Block() as blk:
            @blk.sync
            def _(e):
                sp.play(e)

            @blk.scalar
            def _(e):
                act.play(e)

            @blk.vector
            def _(e):
                dve.play(e)

            @blk.gpsimd
            def _(e):
                pool.play(e)

            @blk.tensor
            def _(e):
                pe.play(e)


def tiles(w):
    k, n = w.shape
    return w.reshape(k // P, P, n // P, P).transpose(2, 0, 1, 3).reshape(-1, P, P)


def wide(w):
    k, n = w.shape
    return w.reshape(k // P, P, n // T, 2, P).transpose(2, 0, 3, 1, 4).reshape(-1, P, P)


def units(*blocks):
    b = np.concatenate(blocks)
    return np.ascontiguousarray(b.reshape(-1, 16, P, P).transpose(0, 2, 1, 3)).reshape(-1, P, UNIT)


def pairs(*ws):
    n = ws[0].shape[1]
    return [tiles(w[:, c:c + T]) for c in range(0, n, T) for w in ws]


def ffn_units(gate, up, down):
    out = []
    for a0, a1 in PARTS:
        out += pairs(gate[:, a0 * P:a1 * P], up[:, a0 * P:a1 * P])
        out.append(tiles(down[a0 * P:a1 * P]))
    return units(*out)


def columns(v):
    return np.ascontiguousarray(v.reshape(-1, P).T)


def layout(a):
    f = np.float32
    w = a["w_in"][0]
    z, xs, bc = w[:, 0:2048], w[:, 2048:4096], w[:, 4096:5120]
    dt = np.concatenate([w[:, 5120:5152], np.zeros((2048, 96), f)], axis=1)
    su, sb_, sc = w[:, 5152:7200], w[:, 7200:9248], w[:, 9248:11296]
    d = {}
    d["w_in"] = units(*pairs(su, sc, sb_), tiles(bc), tiles(dt), tiles(xs), tiles(z))
    d["w_out"] = units(tiles(a["w_out"][0][2048:]), tiles(a["w_out"][0][:2048]))
    d["w_k"], d["w_v"], d["w_q"] = units(tiles(a["w_k"][0])), units(wide(a["w_v"][0])), units(tiles(a["w_q"][0]))
    d["w_o"] = units(tiles(a["w_o"][0]))
    d["ffn"] = ffn_units(a["w_gate"][0], a["w_up"][0], a["w_down"][0])
    q = a["w_qkv_2"][0]
    parts, at = [], 0
    for n in (1024, 512, 512):
        parts += [tiles(q[:, at:at + 2 * n]), wide(q[:, at + 2 * n:at + 3 * n])]
        at += 3 * n
    d["w_qkv_2"] = units(*parts)
    d["w_o_2"] = units(tiles(a["w_o_2"][0][:1024]), tiles(a["w_o_2"][0][1024:]))
    d["ffn_2"] = ffn_units(a["w_gate_2"][0], a["w_up_2"][0], a["w_down_2"][0])

    def fm(x):
        return np.ascontiguousarray(x.reshape(T, 16, P).transpose(2, 1, 0)).reshape(P, 16 * T)

    d["x"], d["mem"] = fm(a["x"]), fm(a["mem"])
    vec = np.zeros((P, NVEC), f)
    for name, (o, n) in VOFF.items():
        if name in ("a_log", "d_skip"):
            v = np.broadcast_to(a[name].reshape(1, 32), (P, 32))
        elif name == "dt_bias":
            v = np.concatenate([a[name].reshape(32), np.zeros(96, f)]).reshape(P, 1)
        elif name in ("eps5", "eps6"):
            v = np.full((P, 1), 1e-5 if name == "eps5" else 1e-6, f)
        else:
            v = columns(a[name])
        vec[:, o:o + n] = v
    d["vec"] = vec
    i = np.arange(P)
    le = (i[:, None] <= i[None, :]).astype(f)
    one = np.ones((P, P), f)
    d["c1"] = np.concatenate([np.eye(P, dtype=f), le, one, one, np.where(le > 0, 0, NEG).astype(f)], axis=1)
    lt = (i[:, None] < i[None, :]).astype(f)
    cm = np.concatenate([lt, one, lt], axis=1)
    qi, ki = i[:, None], np.arange(T)[None, :]
    d0 = np.where(ki[:, :P] // 64 <= qi // 64, -np.abs(qi - ki[:, :P]), NEG)
    d1 = np.where(ki // 64 <= (qi + P) // 64, -np.abs(qi + P - ki), NEG)
    mc = np.where(np.broadcast_to(qi < 64, (P, 64)), NEG, 0.0)
    lam = np.concatenate([a[n].reshape(1, 64) for n in ("lambda_q1_2", "lambda_k1_2", "lambda_q2_2", "lambda_k2_2")], axis=1)
    bd = (i[:, None] // 64 == i[None, :] // 64).astype(f)
    d["c2"] = np.concatenate([bd, le.T, np.eye(P, dtype=f)[::-1], -cm, cm, d0, d1, mc, np.broadcast_to(lam, (P, 256))],
                             axis=1).astype(f)
    d["rel"] = np.ascontiguousarray(a["rel_bias_2"][0][:, ::-1])
    return d


def kernel(**inputs):
    import concourse.bacc as _bacc
    from concourse import mybir as _mybir
    from concourse.bass_utils import run_bass_kernel_spmd as _run

    d = layout({k: np.asarray(v) for k, v in inputs.items()})
    nc = _bacc.Bacc("TRN2", target_bir_lowering=False, num_devices=1)
    arrays, aps = {}, {}
    for name, v in d.items():
        arrays[f"in_{name}"] = v
        aps[name] = nc.dram_tensor(f"in_{name}", v.shape, _mybir.dt.float32, kind="ExternalInput").ap()
    out = nc.dram_tensor("out_0", [P, 16 * T], _mybir.dt.float32, kind="ExternalOutput").ap()
    build(nc, aps, out)
    r = _run(nc, [arrays], core_ids=[0])
    y = r.results[0]["out_0"]
    return np.ascontiguousarray(y.reshape(P, 16, T).transpose(2, 1, 0)).reshape(1, T, 16 * P)
```

```python
from contextlib import ExitStack

import numpy as np

import concourse.bass as bass
from concourse import mybir

F32 = mybir.dt.float32
F32R = mybir.dt.float32r
ALU = mybir.AluOpType
ACT = mybir.ActivationFunctionType
AX = mybir.AxisListType.X

P = 128
T = 256
BLK = 128
SUB = 8 * BLK
UNIT = 2 * SUB
NRAW = 3
NW = 4
NEG = -1e30
LN = 5
LN_EXP = 6

PARTS = [(0, 16), (16, 32), (32, 44)]

VEC = [
    ("norm_mix", 16), ("ssd_conv_w", 96), ("ssd_conv_b", 24), ("sc_conv_w", 48), ("sc_norm", 16),
    ("ssd_norm", 16), ("norm_xa", 16), ("mem_norm", 16), ("norm_ffn", 16), ("norm_final", 16),
    ("attn_norm_2", 16), ("diff_subln_2", 1), ("sb_norm_2", 4), ("ch_norm_2", 4), ("ffn_norm_2", 16),
    ("conv_w_2", 132), ("conv_b_2", 44), ("final_norm_2", 16), ("dt_bias", 1), ("a_log", 32),
    ("d_skip", 32), ("eps5", 1), ("eps6", 1),
]
VOFF = {}
_o = 0
for _n, _w in VEC:
    VOFF[_n] = (_o, _w)
    _o += _w
NVEC = _o

C1 = [("ident", 128), ("tri", 384), ("mneg", 128)]
C2 = [("bd", 128), ("tri2", 128), ("flip", 128), ("nm", 384), ("cm", 384), ("dist", 384), ("mc", 64), ("lam", 256)]
C2_KEPT = 1152


def offsets(table):
    out, at = {}, 0
    for name, w in table:
        out[name] = (at, w)
        at += w
    return out, at


C1OFF, NC1 = offsets(C1)
C2OFF, NC2 = offsets(C2)

UNITS = [("w_in", 89), ("w_out", 32), ("w_q", 4), ("w_k", 4), ("w_v", 4), ("w_o", 4), ("ffn", 132),
         ("w_qkv_2", 48), ("w_o_2", 16), ("ffn_2", 132)]


class Bound:

    def matmul(self, *a, **k):
        return lambda e: e.matmul(*a, **k)

    def transpose(self, *a, **k):
        return lambda e: e.transpose(*a, **k)

    def activation(self, out, in_, func, **k):
        self.func = func
        return lambda e: e.activation(out, in_, func, **k)

    def tensor_tensor(self, *a, **k):
        return lambda e: e.tensor_tensor(*a, **k)

    def tensor_scalar(self, *a, **k):
        return lambda e: e.tensor_scalar(*a, **k)

    def scalar_tensor_tensor(self, *a, **k):
        return lambda e: e.scalar_tensor_tensor(*a, **k)

    def tensor_reduce(self, *a, **k):
        return lambda e: e.tensor_reduce(*a, **k)

    def tensor_copy(self, *a, **k):
        return lambda e: e.tensor_copy(*a, **k)

    def reciprocal(self, *a, **k):
        return lambda e: e.reciprocal(*a, **k)


BOUND = Bound()


class Engine:

    def __init__(self, sem):
        self.sem, self.n, self.todo = sem, 0, []
        self.tables = None

    def __call__(self, fn, *waits, sig=True):
        if sig:
            self.n += 1
        BOUND.func = None
        bound = fn and fn(BOUND)
        if BOUND.func == ACT.Exp and self.tables != LN_EXP or BOUND.func == ACT.Ln and self.tables is None:
            self.load(LN_EXP)
        elif BOUND.func == ACT.Silu:
            self.tables = None
        self.todo.append((waits, bound, self.sem if sig else None))
        return (self.sem, self.n)

    def load(self, tables):
        self.tables = tables
        self.todo.append(((), lambda e: e.add_instruction(mybir.InstLoadActFuncSet(
            name=e.bass.get_next_instruction_name(), ins=[], outs=[], act_func_set_id=tables)), None))

    def dma(self, out, in_, sem, *waits):
        self.todo.append((waits, lambda e: e.dma_start(out, in_).then_inc(sem, 16), None))

    def play(self, e):
        seen = {}
        for waits, fn, sem in self.todo:
            need = {}
            for s, v in waits:
                if v > seen.get(s, 0) and v > need.get(s, 0):
                    need[s] = v
            for s, v in need.items():
                e.wait_ge(s, v)
                seen[s] = v
            if fn is None:
                continue
            ins = fn(e)
            if sem is not None:
                ins.then_inc(sem, 1)


class Pool:

    def __init__(self, bufs):
        self.free = [(b, ()) for b in bufs]

    def get(self):
        return self.free.pop(0)

    def put(self, buf, *toks):
        self.free.append((buf, toks))


class Operand:

    def __init__(self, t):
        self.t = t
        self.tok = [()] * 16
        self.free = ()

    def hi(self, k, n=1):
        return self.t[:, 0, k * T:(k + n) * T]

    def lo(self, k, n=1):
        return self.t[:, 1, k * T:(k + n) * T]


def build(nc, d, out):
    ctx = ExitStack()
    with ctx:
        def sb(name, shape, dt=F32):
            return ctx.enter_context(nc.sbuf_tensor(name, shape, dt))

        def sem(name):
            return ctx.enter_context(nc.semaphore(name))

        raw = sb("raw", [P, NRAW, UNIT])
        whi = sb("whi", [P, NW, SUB], F32R)
        wlo = sb("wlo", [P, NW, SUB], F32R)
        X = sb("X", [P, 16 * T])
        H = Operand(sb("H", [P, 2, 16 * T], F32R))
        Y = Operand(sb("Y", [P, 2, 16 * T], F32R))
        CR = sb("CR", [P, 640], F32R)
        ADT = sb("ADT", [P, 4, 32], F32R)
        AR = sb("AR", [P, 17352])
        PS = ctx.enter_context(nc.psum_tensor("PS", [P, 8, 512], F32))

        pe, act, dve, pool, sp = (Engine(sem(n)) for n in ("s_pe", "s_act", "s_dve", "s_pool", "s_sp"))
        s_w = [sem(f"s_w{i}") for i in range(NRAW)]
        s_x = [sem(f"s_x{i}") for i in range(4)]
        s_c, s_v, s_m, s_c2, s_g, s_h, s_out = (sem(n) for n in ("s_c", "s_v", "s_m", "s_c2", "s_g", "s_h", "s_out"))

        def xt(k, n=1):
            return X[:, k * T:(k + n) * T]

        G0 = 12288
        vec = AR[:, G0:G0 + NVEC]
        c1 = AR[:, G0 + NVEC:G0 + NVEC + NC1]
        g1 = G0 + NVEC + NC1
        SM = AR[:, g1:g1 + 512]
        g1 += 512
        g_bufs = [AR[:, g1 + 512 * i:g1 + 512 * i + 512] for i in range(6)]

        def col(name, i=0):
            o = VOFF[name][0] + i
            return vec[:, o:o + 1]

        def cst(name):
            o, w = C1OFF[name]
            return c1[:, o:o + w]

        ident, tri = cst("ident"), cst("tri")
        ones = tri[:, 128:256]
        TRIr, MNr, Ir = CR[:, 0:384], CR[:, 384:512], CR[:, 512:640]

        acc = Pool([PS[:, i, :] for i in range(4)])
        misc = Pool([PS[:, i, :] for i in range(4, 8)])
        tmp = Pool(list(g_bufs))

        order = [(name, i) for name, n in UNITS for i in range(n)]
        n_sub = 2 * len(order)
        hi_tok, lo_tok, done = {}, {}, {}
        state = {"load": 0, "split": 0, "blk": 0}

        def load():
            u = state["load"]
            if u >= len(order):
                return
            state["load"] += 1
            name, i = order[u]
            waits = (lo_tok[2 * (u - NRAW) + 1],) if u >= NRAW else ()
            sp.dma(raw[:, u % NRAW, :], d[name][i], s_w[u % NRAW], *waits)

        def split():
            s = state["split"]
            if s >= n_sub:
                return
            state["split"] += 1
            u = s // 2
            src = raw[:, u % NRAW, (s % 2) * SUB:(s % 2 + 1) * SUB]
            landed = (s_w[u % NRAW], 16 * (u // NRAW + 1))
            used = (done[s - NW],) if s >= NW else ()
            b = s % NW
            hi_tok[s] = act(lambda e: e.activation(whi[:, b, :], src, ACT.Copy), landed, *used)
            lo_tok[s] = dve(lambda e: e.tensor_tensor(wlo[:, b, :], src, whi[:, b, :].bitcast(F32), ALU.subtract),
                            hi_tok[s], landed, *used)
            if s % 2:
                load()

        active, queue = [], []

        room = [3]

        def holding(n, task, apart=1):
            return n, task, apart

        since = [0]

        def step(width=4):
            since[0] += 1
            if queue and len(active) < width and queue[0][0] <= room[0] and queue[0][2] <= since[0]:
                n, g, _ = queue.pop(0)
                room[0] -= n
                since[0] = 0
                active.append((n, g))
            for n, g in list(active):
                try:
                    next(g)
                except StopIteration:
                    active.remove((n, g))
                    room[0] += n

        def pause(n):
            for _ in range(n):
                yield

        def spare():
            while not misc.free:
                yield
            return misc.get()

        def drain():
            while queue or active:
                step()

        def mm(out_, l, r, start, stop, *waits, sig=False):
            return pe(lambda e: e.matmul(out_, l, r, start=start, stop=stop), *waits, sig=sig)

        def block(width, outs, pairs, first, last, waits):
            b = state["blk"]
            s, o = b // 8, (b % 8) * BLK
            state["blk"] = b + width
            ws = (hi_tok[s], lo_tok[s]) + tuple(waits)
            wh, wl = whi[:, s % NW, o:o + width * BLK], wlo[:, s % NW, o:o + width * BLK]
            end = (b + width) % 8 == 0
            tok = None
            for n, (out_, (xh, xl)) in enumerate(zip(outs, pairs)):
                ops = [(wh, xh), (wh, xl), (wl, xh)] if width == 1 else [(xh, wh), (xl, wh), (xh, wl)]
                for i, (l, r) in enumerate(ops):
                    sig = i == 2 and n == len(outs) - 1 and (end or last)
                    tok = mm(out_, l, r, first and i == 0, last and i == 2, *(ws if n == i == 0 else ()), sig=sig)
            if end:
                done[s] = tok
                split()
            if (b + width) % 4 == 0:
                step()
            return tok

        def mtiles(op, K, n=2, k0=0):
            bank, free = acc.get()
            for m in range(n):
                for k in range(K):
                    tok = block(1, [bank[:, m * T:(m + 1) * T]], [(op.hi(k0 + k), op.lo(k0 + k))], k == 0, k == K - 1,
                                op.tok[k0 + k] + (free if k == 0 else ()))
            return bank, tok

        def rows(op):
            (b0, f0), (b1, f1) = acc.get(), acc.get()
            for k in range(16):
                tok = block(2, [b0[:, 0:T], b1[:, 0:T]],
                            [(op.hi(k)[:, t * P:(t + 1) * P], op.lo(k)[:, t * P:(t + 1) * P]) for t in range(2)],
                            k == 0, k == 15, op.tok[k] + ((f0 + f1) if k == 0 else ()))
            return (b0, b1), tok

        def halves(op, k, n, src, *waits):
            hi, lo = op.hi(k, n), op.lo(k, n)
            a = act(lambda e: e.activation(hi, src, ACT.Copy), *waits, *op.free)
            b = dve(lambda e: e.tensor_tensor(lo, src, hi.bitcast(F32), ALU.subtract), a, *waits, *op.free)
            for i in range(n):
                op.tok[k + i] = (a, b)
            return b

        def root(dst, ms, scale, eps, *waits):
            a = act(lambda e: e.activation(dst, ms, ACT.Ln, bias=eps, scale=scale), *waits)
            return a, act(lambda e: e.activation(dst, dst, ACT.Exp, scale=-0.5), a)

        class Sum:

            def __init__(self):
                self.buf, self.w = tmp.get()
                self.tok = None
                self.apart, self.rest = False, None

            def add(self, src, *waits):
                if self.tok is None:
                    self.tok = act(lambda e: e.activation(self.buf, src, ACT.Square), *waits, *self.w)
                    return self.tok
                q, w = tmp.get()
                a = act(lambda e: e.activation(q, src, ACT.Square), *waits, *w)
                if self.apart:
                    self.rest = (q, a)
                    return a
                self.tok = pool(lambda e: e.tensor_tensor(self.buf, self.buf, q, ALU.add), a, self.tok)
                tmp.put(q, self.tok)
                return a

        class Norm:

            def __init__(self, s, eps, r, cols=None, free=()):
                self.s, self.eps, self.r, self.cols, self.free, self.ok = s, eps, r, cols, free, None

            def task(self, lag=4):
                yield from pause(lag)
                s = self.s
                bank, f = yield from spare()
                mm(bank[:, 0:T], ones, s.buf[:, 0:T], True, False, s.tok, *f)
                t = mm(bank[:, 0:T], ones, s.buf[:, T:2 * T], False, s.rest is None, sig=True)
                if s.rest is not None:
                    q, a = s.rest
                    mm(bank[:, 0:T], ones, q[:, 0:T], False, False, a)
                    t = mm(bank[:, 0:T], ones, q[:, T:2 * T], False, True, sig=True)
                    tmp.put(q, t)
                f = ()
                if self.cols is not None:
                    for i in range(2):
                        mm(bank[:, T + i:T + i + 1], s.buf[:, i * P:(i + 1) * P], ones[:, 0:1], True, False)
                        t = mm(bank[:, T + i:T + i + 1], s.buf[:, T + i * P:T + (i + 1) * P], ones[:, 0:1], False, True,
                               sig=True)
                    f = self.refined(self.cols, s.buf[:, 0:2], s.buf[:, 2:4], bank[:, T:T + 2], t)
                c, self.ok = self.refined(self.r, s.buf[:, 0:T], s.buf[:, T:2 * T], bank[:, 0:T], t, *f, *self.free)
                misc.put(bank, c)
                tmp.put(s.buf, self.ok)

            def refined(self, r, m, u, bank, *waits):
                u = u[:, 0:m.shape[-1]]
                c = dve(lambda e: e.tensor_scalar(m, bank, 1.0 / 2048, self.eps, ALU.mult, ALU.add), *waits)
                a, b = root(r, m, 1.0, 0.0, c, *waits)
                k = dve(lambda e: e.scalar_tensor_tensor(u, r, -0.5, m, ALU.mult, ALU.mult), b)
                k = dve(lambda e: e.tensor_tensor(u, u, r, ALU.mult), k)
                return c, dve(lambda e: e.scalar_tensor_tensor(r, u, 1.5, r, ALU.add, ALU.mult), k)

        def need(n):
            while n.ok is None:
                step()
            return n.ok

        def both(r):
            return r.unsqueeze(1).to_broadcast([P, 2, T])

        def two(x):
            return x.rearrange("p (a b) -> p a b", a=2)

        def times(dst, src, r, *waits):
            return dve(lambda e: e.tensor_tensor(two(dst), two(src), both(r), ALU.mult), *waits)

        def gained(op, k, src, gain, *waits):
            hi, lo, g = op.hi(k), op.lo(k), col(gain, k) if isinstance(gain, str) else gain[:, k:k + 1]
            a = act(lambda e: e.activation(hi, src, ACT.Copy, scale=g), *waits, *op.free)
            b = dve(lambda e: e.scalar_tensor_tensor(lo, src, g, hi.bitcast(F32), ALU.mult, ALU.subtract), a, *waits, *op.free)
            op.tok[k] = (a, b)

        def load_x(i):
            sp.dma(xt(4 * i, 4), d["x"][:, 4 * i * T:(4 * i + 4) * T], s_x[i])

        act.dma(vec, d["vec"], s_v)
        load_x(0)
        load()
        for i in range(1, 4):
            load_x(i)
        load()
        load()
        act.dma(c1, d["c1"], s_c)
        C_OK, V_OK = (s_c, 16), (s_v, 16)
        split()
        dve(None, V_OK, sig=False)
        act(None, V_OK, sig=False)
        for k in range(16):
            if k == 4:
                split()
            gained(H, k, xt(k), "norm_mix", (s_x[k // 4], 16))
        split()
        split()
        cr0 = dve(lambda e: e.tensor_copy(CR[:, 0:384], tri), C_OK)
        cr1 = dve(lambda e: e.tensor_copy(MNr, cst("mneg")))
        cr2 = dve(lambda e: e.tensor_copy(Ir, ident))
        RN, RSQ, RN2 = AR[:, 17096:17352], SM[:, 224:480], SM[:, 224:480]
        sx = Sum()
        nx = Norm(sx, col("eps5"), RN)

        def first_squares():
            for k in range(0, 16, 2):
                sx.add(xt(k, 2), (s_x[k // 4], 16))
                if k % 4:
                    yield
            pe(None, cr2, C_OK, sig=False)
            yield from nx.task(6)

        queue.append(holding(1, first_squares()))
        rsq = []

        mix = [AR[:, o:o + 512] for o in range(9728, G0, 512)]
        for b in mix:
            tmp.put(b)
        room[0] += 4
        Z, XS, CB = AR[:, 0:4096], AR[:, 4096:8192], AR[:, 8192:9728]

        def conv(dst, src, taps, bias, waits, width):
            w = [lambda i=i: taps(i) for i in range(width)]
            last = w[width - 1]()
            if bias is None:
                t = dve(lambda e: e.tensor_scalar(dst[:, 0:T], src[:, 0:T], last, None, ALU.mult), *waits)
            else:
                t = dve(lambda e: e.tensor_scalar(dst[:, 0:T], src[:, 0:T], last, bias, ALU.mult, ALU.add), *waits)
            for sh in range(1, width):
                wi = w[width - 1 - sh]()
                t = dve(lambda e, sh=sh, wi=wi: e.scalar_tensor_tensor(
                    dst[:, sh:T], src[:, 0:T - sh], wi, dst[:, sh:T], ALU.mult, ALU.add), t)
            return t

        def sc_norm(j, v, vt):
            q, w = tmp.get()
            a = act(lambda e: e.activation(q, v, ACT.Square), vt, *w)
            yield from pause(4)
            bank, f = yield from spare()
            t = mm(bank, ones, q, True, True, a, *f, sig=True)
            a1, rt = root(q, bank, 1.0 / 128, col("eps5"), t)
            misc.put(bank, a1)
            for i in range(2):
                c = dve(lambda e, i=i: e.scalar_tensor_tensor(
                    v[:, i * T:(i + 1) * T], v[:, i * T:(i + 1) * T], col("sc_norm", 2 * j + i), q[:, i * T:(i + 1) * T],
                    ALU.mult, ALU.mult), rt, vt)
            tmp.put(q, c)
            tmp.put(v, halves(Y, 2 * j, 2, v, c))

        for j in range(8):
            bu, tu = mtiles(H, 16)
            u, w = tmp.get()
            bc, tc = mtiles(H, 16)
            if j == 0:
                rsq.append(dve(lambda e: e.tensor_tensor(RSQ, RN, RN, ALU.mult), need(nx)))
            a = times(u, bu, RSQ, tu, rsq[0], *w)
            acc.put(bu, a)
            c = dve(lambda e, u=u, bc=bc: e.tensor_tensor(u, bc, u, ALU.mult), tc, a)
            acc.put(bc, c)
            v, w = tmp.get()
            for i in range(2):
                vt = conv(v[:, i * T:(i + 1) * T], u[:, i * T:(i + 1) * T],
                          lambda n, i=i, j=j: col("sc_conv_w", n * 16 + 2 * j + i), None, (c,) + w, 3)
            tmp.put(u, vt)
            vt = times(v, v, RN, vt)
            bb, tb = mtiles(H, 16)
            vt = dve(lambda e, v=v, bb=bb: e.tensor_tensor(v, bb, v, ALU.mult), tb, vt)
            acc.put(bb, vt)
            queue.append(holding(1, sc_norm(j, v, vt)))

        def xbc(i0, dst, ready, *waits):
            bank, t = mtiles(H, 16)
            u, w = tmp.get()
            t = times(u, bank, RN, t, *w)
            acc.put(bank, t)
            q, w = tmp.get()
            for i in range(2):
                ct = conv(q[:, i * T:(i + 1) * T], u[:, i * T:(i + 1) * T],
                          lambda n, i=i: col("ssd_conv_w", n * 24 + i0 + i), col("ssd_conv_b", i0 + i), (t,) + w, 4)
            tmp.put(u, ct)
            a = act(lambda e: e.activation(dst if dst is not None else q, q, ACT.Silu), ct, *waits)
            if dst is not None:
                tmp.put(q, a)
            return q, a

        for i in range(4):
            _, bc_tok = xbc(16 + 2 * i, Z[:, i * 512:(i + 1) * 512], None)
        BM, CM_ = Z[:, 0:1024], Z[:, 1024:2048]
        cb_tok = [None] * 4

        def cb_task():
            yield from pause(6)
            for g in range(4):
                bank, f = yield from spare()
                mm(bank[:, 0:256], BM[:, g * T:g * T + 128], CM_[:, g * T:(g + 1) * T], True, True, bc_tok, *f)
                t = mm(bank[:, 256:384], BM[:, g * T + 128:(g + 1) * T], CM_[:, g * T + 128:(g + 1) * T], True, True, sig=True)
                cb_tok[g] = act(lambda e, g=g, bank=bank: e.activation(CB[:, g * 384:(g + 1) * 384], bank[:, 0:384], ACT.Copy), t)
                misc.put(bank, cb_tok[g])
                yield

        queue.append(holding(0, cb_task()))
        bdt, tdt = mtiles(H, 16, 1)
        dtT = SM[:, 0:64]
        nacs = SM[:, 64:128]
        arow = SM[:, 128:160]
        adt = SM[:, 160:224]
        ssd_ready = []

        def dt_task():
            x, w = tmp.get()
            y, w2 = tmp.get()
            xv, ab, e1, u1 = (q[0:32, :] for q in (x[:, 0:T], x[:, T:2 * T], y[:, 0:T], y[:, T:2 * T]))
            c = dve(lambda e: e.tensor_tensor(xv, bdt[0:32, 0:T], RN[0:32, :], ALU.mult), tdt, *w, *w2)
            acc.put(bdt, c)
            ar = act(lambda e: e.activation(arow, vec[:, VOFF["a_log"][0]:VOFF["a_log"][0] + 32], ACT.Exp))
            c = dve(lambda e: e.tensor_scalar(xv, xv, col("dt_bias")[0:32, :], None, ALU.add), c)
            a = act(lambda e: e.activation(ab, xv, ACT.Abs), c)
            a = act(lambda e: e.activation(e1, ab, ACT.Exp, scale=-1.0), a)
            c1_ = dve(lambda e: e.tensor_scalar(u1, e1, 1.0, None, ALU.add), a)
            act.load(LN)
            a = act(lambda e: e.activation(ab, u1, ACT.Ln), c1_)
            yield from pause(2)
            c = dve(lambda e: e.tensor_scalar(u1, u1, -1.0, None, ALU.add), a)
            m, wm = tmp.get()
            mk, rc = m[0:32, 0:T], m[0:32, T:2 * T]
            c = dve(lambda e: e.tensor_scalar(mk, u1, 0.0, None, ALU.is_equal), c, *wm)
            yield
            k1 = dve(lambda e: e.tensor_tensor(u1, u1, mk, ALU.add), c)
            k2 = dve(lambda e: e.tensor_tensor(ab, ab, mk, ALU.add), c)
            k3 = dve(lambda e: e.reciprocal(rc, u1), k1)
            k4 = dve(lambda e: e.tensor_tensor(ab, ab, e1, ALU.mult), k2)
            k5 = dve(lambda e: e.tensor_tensor(ab, ab, rc, ALU.mult), k3, k4)
            k6 = dve(lambda e: e.scalar_tensor_tensor(xv, xv, 0.0, ab, ALU.max, ALU.add), k5)
            yield from pause(7)
            bank, f = yield from spare()
            for t in range(2):
                tt = pe(lambda e, t=t: e.transpose(bank[:, t * 32:(t + 1) * 32], xv[:, t * P:(t + 1) * P], ident[0:32, 0:32]),
                        k6, *f)
            c = dve(lambda e: e.tensor_copy(dtT, bank[:, 0:64]), tt)
            misc.put(bank, c)
            tmp.put(x, tt)
            tmp.put(y, k6)
            tmp.put(m, k6)
            for t in range(2):
                c2 = dve(lambda e, t=t: e.scalar_tensor_tensor(adt[:, t * 32:(t + 1) * 32], dtT[:, t * 32:(t + 1) * 32], -1.0,
                                                                 arow, ALU.mult, ALU.mult), c, ar)
            h = dve(lambda e: e.tensor_copy(ADT[:, 0:2, :], adt), c2)
            l = dve(lambda e: e.tensor_tensor(ADT[:, 2:4, :], adt, ADT[:, 0:2, :].bitcast(F32).rearrange("p a b -> p (a b)"),
                                              ALU.subtract), h)
            yield from pause(7)
            bank, f = yield from spare()
            mm(bank[:, 0:32], tri[:, 0:128], adt[:, 0:32], True, True, c2, *f)
            mm(bank[:, 32:64], ones, adt[:, 0:32], True, False)
            t = mm(bank[:, 32:64], tri[:, 0:128], adt[:, 32:64], False, True, sig=True)
            c = dve(lambda e: e.tensor_scalar(nacs, bank[:, 0:64], -1.0, None, ALU.mult), t)
            misc.put(bank, c)
            ssd_ready.extend([c, l])

        queue.append(holding(3, dt_task()))
        xs_tok = [None] * 8

        def xs_task(j, q, a):
            yield from pause(6)
            bank, f = yield from spare()
            for t in range(2):
                for i in range(2):
                    tt = pe(lambda e, t=t, i=i: e.transpose(bank[:, t * T + i * P:t * T + (i + 1) * P],
                                                              q[:, i * T + t * P:i * T + (t + 1) * P], ident), a, *f)
            dst = XS.rearrange("p (t n) -> p t n", t=2)[:, :, j * T:(j + 1) * T]
            xs_tok[j] = act(lambda e: e.activation(dst, bank.rearrange("p (t n) -> p t n", t=2), ACT.Copy), tt)
            misc.put(bank, xs_tok[j])
            tmp.put(q, tt)

        for j in range(8):
            q, a = xbc(2 * j, None, None)
            queue.append(holding(0, xs_task(j, q, a)))
        while None in cb_tok:
            step()
        z_tok = [None] * 16
        def ssd_pair(i):
            while len(ssd_ready) < 2 or xs_tok[i // 2] is None:
                yield
            es = []
            for h in (2 * i, 2 * i + 1):
                g = h // 8
                bank, f = yield from spare()
                w0 = [ADT[:, 2 * p, h:h + 1].to_broadcast([P, P]) for p in range(2)]
                w1 = [ADT[:, 2 * p + 1, h:h + 1].to_broadcast([P, P]) for p in range(2)]
                mm(bank[:, 0:384], w0[0], TRIr, True, False, *ssd_ready, *f)
                mm(bank[:, 0:384], w0[1], TRIr, False, False)
                for p in range(2):
                    for o in (128, 256):
                        mm(bank[:, o:o + 128], w1[p], TRIr[:, 0:128], False, False)
                mm(bank[:, 0:128], Ir, MNr, False, False)
                t = mm(bank[:, 256:384], Ir, MNr, False, True, sig=True)
                E, w = tmp.get()
                a0 = act(lambda e, h=h, E=E, bank=bank: e.activation(E[:, 0:256], bank[:, 0:256], ACT.Exp,
                                                                       bias=nacs[:, h:h + 1]), t, *w, *ssd_ready)
                a1 = act(lambda e, h=h, E=E, bank=bank: e.activation(E[:, 256:384], bank[:, 256:384], ACT.Exp,
                                                                       bias=nacs[:, 32 + h:33 + h]))
                misc.put(bank, a1)
                cb = CB[:, g * 384:(g + 1) * 384]
                c0 = dve(lambda e, h=h, E=E, cb=cb: e.scalar_tensor_tensor(
                    E[:, 0:256], cb[:, 0:256], dtT[:, h:h + 1], E[:, 0:256], ALU.mult, ALU.mult), a0, cb_tok[g])
                c1_ = dve(lambda e, h=h, E=E, cb=cb: e.scalar_tensor_tensor(
                    E[:, 256:384], cb[:, 256:384], dtT[:, 32 + h:33 + h], E[:, 256:384], ALU.mult, ALU.mult), a1)
                for o, cc in ((0, c0), (256, c1_)):
                    c = dve(lambda e, h=h, E=E, o=o: e.scalar_tensor_tensor(
                        E[:, o:o + 128], ident, col("d_skip", h), E[:, o:o + 128], ALU.mult, ALU.add), cc)
                es.append((h, E, c))
            yield from pause(6)
            while z_tok[i] is None:
                yield
            bank, f = yield from spare()
            for h, E, c in es:
                o = bank[64 * (h % 2):64 * (h % 2) + 64, 0:T]
                mm(o, XS[:, 64 * h:64 * h + 64], E[:, 0:256], True, False, c, xs_tok[h // 4], *f)
                t = mm(o[:, 128:256], XS[:, 2048 + 64 * h:2048 + 64 * h + 64], E[:, 256:384], False, True, sig=True)
                tmp.put(E, t)
            zt = Z[:, i * T:(i + 1) * T]
            z_tok[i] = dve(lambda e: e.tensor_tensor(zt, bank[:, 0:T], zt, ALU.mult), t, z_tok[i])
            misc.put(bank, z_tok[i])
            pair_done[i] = True

        def ssd_group(g):
            while not all(pair_done[4 * g:4 * g + 4]):
                yield
            zs = [Z[:, (4 * g + 2 * p) * T:(4 * g + 2 * p + 2) * T] for p in range(2)]
            qs = []
            for p in range(2):
                q, w = tmp.get()
                a = act(lambda e, p=p, q=q: e.activation(q, zs[p], ACT.Square), z_tok[4 * g + 2 * p], z_tok[4 * g + 2 * p + 1], *w)
                qs.append(q)
            yield from pause(4)
            bank, f = yield from spare()
            for n in range(4):
                t = mm(bank[:, 0:T], ones, qs[n // 2][:, (n % 2) * T:(n % 2 + 1) * T], n == 0, n == 3, a, *f, sig=n == 3)
            r = qs[0][:, 0:T]
            a1, rt = root(r, bank[:, 0:T], 1.0 / 512, col("eps5"), t)
            misc.put(bank, a1)
            tmp.put(qs[1], t)
            yield from pause(2)
            while not z_all or len(z_end) < g:
                yield
            for p in range(2):
                for i in range(2):
                    k = 4 * g + 2 * p + i
                    c = dve(lambda e, k=k: e.scalar_tensor_tensor(
                        Z[:, k * T:(k + 1) * T], Z[:, k * T:(k + 1) * T], col("ssd_norm", k), r, ALU.mult, ALU.mult),
                        rt, z_tok[k])
                yield
                last = halves(H, 4 * g + 2 * p, 2, zs[p], c)
                yield
            tmp.put(qs[0], c)
            z_end.append(last)

        pair_done, z_all, z_end = [False] * 16, [], []
        for g in range(4):
            for i in range(4):
                queue.append(holding(2, ssd_pair(4 * g + i)))
        for g in range(4):
            queue.append(holding(2, ssd_group(g)))
        for j in range(8):
            bank, t = mtiles(H, 16)
            zj = Z[:, j * 512:(j + 1) * 512]
            c = times(zj, bank, RN, t, *cb_tok)
            acc.put(bank, c)
            a = act(lambda e, zj=zj: e.activation(zj, zj, ACT.Silu), c)
            z_tok[2 * j] = z_tok[2 * j + 1] = a
        H.free = (t,)

        z_all.append(t)

        def residual(bank, t, j, s=None, op=None, gain=None):
            c = dve(lambda e: e.tensor_tensor(xt(2 * j, 2), xt(2 * j, 2), bank, ALU.add), t)
            acc.put(bank, c)
            if op is not None:
                for i in range(2):
                    gained(op, 2 * j + i, xt(2 * j + i), gain, c)
            if s is not None:
                s.add(xt(2 * j, 2), c)

        for j in range(8):
            bank, t = mtiles(Y, 16)
            residual(bank, t, j)
        Y.free = (t,)
        drain()

        act.dma(XS, d["mem"], s_m, t, *[z_tok[i] for i in range(16)])

        mcol = SM[:, 200:202]
        sm = Sum()
        rmb, rmw = tmp.get()
        nm = Norm(sm, col("eps5"), rmb[:, 0:T], mcol, rmw)

        def mem_squares():
            yield from pause(14)
            for k in range(0, 16, 2):
                sm.add(XS[:, k * T:(k + 2) * T], (s_m, 16))
                yield
            yield from nm.task()

        def mem_operand():
            for k in range(16):
                gained(H, k, XS[:, k * T:(k + 1) * T], "mem_norm", (s_m, 16))
                if k % 2:
                    yield

        queue.append(holding(1, mem_squares()))
        sx = Sum()
        for j in range(8):
            bank, t = mtiles(H, 16)
            residual(bank, t, j, sx, Y, "norm_xa")
        H.free = (t,)
        drain()

        nx = Norm(sx, col("eps5"), RN)
        queue.append(holding(0, nx.task(5)))
        queue.append(holding(0, mem_operand()))
        KT, VM, QT = Z[:, 0:1024], Z[:, 1024:2048], Z[:, 2048:3072]
        for j in range(2):
            bank, t = mtiles(Y, 16)
            dst = QT[:, j * 512:(j + 1) * 512]
            q_tok = dve(lambda e, bank=bank, dst=dst: e.scalar_tensor_tensor(
                two(dst), two(bank), 128.0 ** -0.5, both(RN), ALU.mult, ALU.mult), t, need(nx), *z_end)
            acc.put(bank, q_tok)
        Y.free = (t,)
        drain()
        for j in range(2):
            bank, t = mtiles(H, 16)
            k_tok = times(KT[:, j * 512:(j + 1) * 512], bank, rmb[:, 0:T], t, nm.ok, *z_end)
            acc.put(bank, k_tok)
        tmp.put(rmb, k_tok)
        v_tok = []
        stat = SM[:, 160:192]

        def xa_head(h):
            st = stat[:, 8 * h:8 * h + 8]
            yield
            bank, f = yield from spare()
            for t in range(2):
                tt = mm(bank[:, t * T:(t + 1) * T], QT[:, h * T + t * P:h * T + (t + 1) * P], KT[:, h * T:(h + 1) * T],
                        True, True, q_tok, k_tok, *f, sig=t == 1)
            yield
            c = dve(lambda e: e.tensor_reduce(st[:, 0:2], bank.rearrange("p (t n) -> p t n", t=2), AX, ALU.max, negate=True), tt)
            yield
            Pb, w = tmp.get()
            for t in range(2):
                a = act(lambda e, t=t: e.activation(Pb[:, t * T:(t + 1) * T], bank[:, t * T:(t + 1) * T], ACT.Exp,
                                                     bias=st[:, t:t + 1], accum_out=st[:, 2 + t:3 + t]), c, *w)
            misc.put(bank, a)
            yield
            c = dve(lambda e: e.reciprocal(st[:, 4:6], st[:, 2:4]), a)
            for t in range(2):
                cn = dve(lambda e, t=t: e.tensor_scalar(Pb[:, t * T:(t + 1) * T], Pb[:, t * T:(t + 1) * T],
                                                        st[:, 4 + t:5 + t], None, ALU.mult), c)
            yield from pause(2)
            bank, f = yield from spare()
            for m in range(2):
                for t in range(2):
                    tt = pe(lambda e, m=m, t=t: e.transpose(bank[:, m * T + t * P:m * T + (t + 1) * P],
                                                              Pb[:, t * T + m * P:t * T + (m + 1) * P], ident), cn, *f)
            yield
            PT, w = tmp.get()
            a = act(lambda e: e.activation(PT, bank, ACT.Copy), tt, *w)
            misc.put(bank, a)
            tmp.put(Pb, tt)
            yield from pause(2)
            while len(v_tok) < 4:
                yield
            yield
            bank, f = yield from spare()
            for m in range(2):
                tt = mm(bank[:, 0:T], VM[:, m * 512 + h * P:m * 512 + (h + 1) * P], PT[:, m * T:(m + 1) * T],
                        m == 0, m == 1, a, *v_tok, *f, sig=m == 1)
            tmp.put(PT, tt)
            misc.put(bank, halves(Y, h, 1, bank[:, 0:T], tt))

        for h in range(4):
            queue.append(holding(1, xa_head(h)))
        for j in range(2):
            banks, t = rows(H)
            for m in range(2):
                v_tok.append(act(lambda e, j=j, m=m, b=banks[m]: e.activation(
                    VM[:, m * 512 + j * T:m * 512 + (j + 1) * T], b[:, 0:T], ACT.Copy, scale=mcol[:, m:m + 1]), t, nm.ok))
                acc.put(banks[m], v_tok[-1])
        H.free = (t,)
        drain()
        c2_free = [t for b, toks in tmp.free if any(b is m for m in mix) for t in toks]
        tmp.free = [x for x in tmp.free if not any(x[0] is m for m in mix)]
        room[0] -= 5
        sx = Sum()
        for j in range(8):
            bank, t = mtiles(Y, 4)
            residual(bank, t, j, sx, H, "norm_ffn")
        Y.free = (t,)

        def ffn(conv2, eps, op, gain):
            s = None
            n = Norm(sx, eps, RN)
            queue.append(holding(0, n.task(5)))
            for a0, a1 in PARTS:
                for j in range(a0, a1, 2):
                    bg, tg = mtiles(H, 16)
                    q, w = tmp.get()
                    tg = times(q, bg, RN, tg, need(n), *w)
                    acc.put(bg, tg)
                    if conv2:
                        u, w = tmp.get()
                        for i in range(2):
                            c = conv(u[:, i * T:(i + 1) * T], q[:, i * T:(i + 1) * T],
                                     lambda m, i=i, j=j: col("conv_w_2", m * 44 + j + i), col("conv_b_2", j + i), (tg,) + w, 3)
                        tmp.put(q, c)
                        q, tg = u, c
                    a = act(lambda e, q=q: e.activation(q, q, ACT.Silu), tg)
                    a = times(q, q, RN, a)
                    bu, tu = mtiles(H, 16)
                    c = dve(lambda e, q=q, bu=bu: e.tensor_tensor(q, bu, q, ALU.mult), tu, a)
                    acc.put(bu, c)
                    tmp.put(q, halves(Y, j - a0, 2, q, c))
                if a1 == 44:
                    H.free = (tu,)
                    s = Sum()
                for j in range(8):
                    bank, t = mtiles(Y, a1 - a0)
                    if s is not None and op is None:
                        s.apart = j == 7
                    residual(bank, t, j, s, op if s is not None else None, gain)
                Y.free = (t,)
            return s

        g12 = SM[:, 480:496]
        g12_tok = dve(lambda e: e.tensor_tensor(g12, vec[:, VOFF["norm_final"][0]:VOFF["norm_final"][0] + 16],
                                                vec[:, VOFF["attn_norm_2"][0]:VOFF["attn_norm_2"][0] + 16], ALU.mult))
        act(None, g12_tok, sig=False)
        dve(None, g12_tok, sig=False)
        c2 = AR[:, 9216:9216 + NC2]
        act.dma(c2, d["c2"], s_c2, *c2_free)

        def k2(name):
            o, w = C2OFF[name]
            return c2[:, o:o + w]

        lam = SM[:, 0:16]
        lv = k2("lam")
        Dr, MCr = CR[:, 0:384], CR[:, 384:448]
        inv, nlam, eps_a, gain_a = lam[:, 7:8], lam[:, 8:9], lam[:, 9:10], lam[:, 10:11]
        dr_tok, mc_tok, lam_ok = [], [], []
        scratch = nc.dram_tensor("rel_rows", [8, 512], F32).ap()
        hank_src = bass.AP(tensor=scratch.tensor, offset=0, ap=[[1, P], [512, 8], [1, 256]])

        def constants():
            G_row, gw = tmp.get()
            g8 = G_row[0:8, :]
            act.dma(g8[:, 127:319], d["rel"], s_g, *gw)
            yield from pause(12)
            C2_OK = (s_c2, 16)
            pe(None, C2_OK, sig=False)
            dve(None, C2_OK, sig=False)
            dr_tok.append(dve(lambda e: e.tensor_copy(Dr, k2("dist"))))
            mc_tok.append(dve(lambda e: e.tensor_copy(MCr, k2("mc"))))
            yield
            q, w = tmp.get()
            for i in range(2):
                c = dve(lambda e, i=i, q=q: e.tensor_tensor(q[:, 64 * i:64 * i + 64], lv[:, 128 * i:128 * i + 64],
                                                            lv[:, 128 * i + 64:128 * i + 128], ALU.mult), *w)
            c = dve(lambda e: e.tensor_reduce(lam[:, 0:2], q[:, 0:128].rearrange("p (a b) -> p a b", a=2), AX, ALU.add), c)
            tmp.put(q, c)
            a = act(lambda e: e.activation(lam[:, 2:4], lam[:, 0:2], ACT.Exp), c)
            yield from pause(3)
            c = dve(lambda e: e.tensor_tensor(lam[:, 4:5], lam[:, 2:3], lam[:, 3:4], ALU.subtract), a)
            c = dve(lambda e: e.tensor_scalar(lam[:, 4:5], lam[:, 4:5], 0.8 - 0.6, None, ALU.add), c)
            c = dve(lambda e: e.tensor_scalar(lam[:, 5:6], lam[:, 4:5], -1.0, None, ALU.mult), c)
            c = dve(lambda e: e.tensor_tensor(lam[:, 6:7], lam[:, 4:5], lam[:, 5:6], ALU.max), c)
            c = dve(lambda e: e.tensor_scalar(lam[:, 6:7], lam[:, 6:7], 1.0, None, ALU.max), c)
            c = dve(lambda e: e.reciprocal(lam[:, 7:8], lam[:, 6:7]), c)
            c0 = dve(lambda e: e.tensor_tensor(lam[:, 8:9], lam[:, 5:6], lam[:, 7:8], ALU.mult), c)
            c1_ = dve(lambda e: e.tensor_tensor(lam[:, 9:10], lam[:, 7:8], lam[:, 7:8], ALU.mult), c)
            c1_ = dve(lambda e: e.tensor_scalar(lam[:, 9:10], lam[:, 9:10], 1e-5, None, ALU.mult), c1_)
            c2_ = dve(lambda e: e.tensor_scalar(lam[:, 10:11], col("diff_subln_2"), 1.0 - (0.8 - 0.6), None, ALU.mult))
            lam_ok.extend([c0, c1_, c2_])
            for i in range(3):
                o = 9216 + C2_KEPT + 512 * i
                tmp.put(AR[:, o:o + 512], dr_tok[0], mc_tok[0], c1_)
            room[0] += 3
            yield
            c = dve(lambda e: e.tensor_copy(g8[:, 0:127], g8[:, 127:128].to_broadcast([8, 127])), (s_g, 16), *gw)
            c = dve(lambda e: e.tensor_copy(g8[:, 319:511], g8[:, 318:319].to_broadcast([8, 192])))
            c = dve(lambda e: e.tensor_copy(g8[:, 511:512], g8[:, 318:319]))
            act.dma(scratch, g8, s_g, c)
            tmp.put(G_row, (s_g, 32))

        queue.append(holding(2, constants()))

        sx = ffn(False, col("eps5"), H, g12)

        n1 = Norm(sx, col("eps5"), RN, SM[:, 496:498])
        s2 = Sum()
        n2 = Norm(s2, col("eps6"), RN2, SM[:, 498:500])
        rr = []

        def middle():
            yield from n1.task(3)
            for k in range(16):
                c = dve(lambda e, k=k: e.scalar_tensor_tensor(xt(k), xt(k), col("norm_final", k), RN, ALU.mult, ALU.mult),
                        n1.ok, *H.tok[k])
                if k % 2:
                    s2.add(xt(k - 1, 2), c)
                    yield
            yield from n2.task(6)
            c = dve(lambda e: e.tensor_tensor(RN, RN, RN2, ALU.mult), n2.ok, c)
            rr.append(dve(lambda e: e.tensor_tensor(SM[:, 496:498], SM[:, 496:498], SM[:, 498:500], ALU.mult), c))

        queue.append(holding(1, middle()))
        QA, KA, VA = AR[:, 0:2048], AR[:, 2048:4096], AR[:, 4096:6144]
        QB, KB, VB = AR[:, 6144:7168], AR[:, 7168:8192], AR[:, 8192:9216]
        QC, KC, VC = AR[:, 0:1024], AR[:, 1024:2048], AR[:, 2048:3072]
        HK = AR[:, 3072:5120]

        def qk(dq, dk, n, *waits, slopes=(1.0,) * 8):
            todo = [(dst, sc, j) for dst, sc in ((dq, 0.125), (dk, 1.0)) for j in range(n // 2)]
            late = 0 if rr else 3
            banks, count = [], len(todo)
            for i in range(count):
                banks.append(mtiles(H, 16))
                if i < late:
                    continue
                while not rr:
                    step()
                for dst, sc, j in [todo.pop(0) for _ in range(min(len(banks), 2) if i < count - 1 else len(banks))]:
                    bank, t = banks.pop(0)
                    for h in (2 * j, 2 * j + 1):
                        o = h * T
                        s_ = sc / slopes[h] if dst is dq else sc
                        b_ = dve(lambda e: e.scalar_tensor_tensor(dst[:, o:o + T], bank[:, o % 512:o % 512 + T], s_, RN,
                                                                  ALU.mult, ALU.mult), t, rr[0], *waits)
                    acc.put(bank, b_)
            return b_, t

        def values(dv, n, *waits):
            for j in range(n // 2):
                banks, t = rows(H)
                for m in range(2):
                    a = act(lambda e, j=j, m=m, b=banks[m]: e.activation(
                        dv[:, m * n * P + j * T:m * n * P + (j + 1) * T], b[:, 0:T], ACT.Copy,
                        scale=SM[:, 496 + m:497 + m]), t, rr[0], *waits)
                    acc.put(banks[m], a)
            return a, t

        slopes = [2.0 ** -(h + 1) for h in range(8)]
        a_tok, t = qk(QA, KA, 8, slopes=slopes)
        room[0] += 3

        def scaled(o_bank, tt, mat, scale, eps, gain, tile, *waits):
            q, w = tmp.get()
            a = act(lambda e: e.activation(q[:, 0:T], o_bank[:, 0:T], ACT.Square), tt, *w, *waits)
            yield from pause(2)
            bank, f = yield from spare()
            t = mm(bank[:, 0:T], mat, q[:, 0:T], True, True, a, *f, sig=True)
            yield
            a1, rt = root(q[:, T:2 * T], bank[:, 0:T], scale, eps, t)
            misc.put(bank, a1)
            yield from pause(2)
            c = dve(lambda e: e.scalar_tensor_tensor(q[:, 0:T], o_bank[:, 0:T], gain, q[:, T:2 * T], ALU.mult, ALU.mult), rt)
            misc.put(o_bank, c)
            yield
            tmp.put(q, halves(Y, tile, 1, q[:, 0:T], c))

        def turn(heads):
            banks = []
            for Wb, wt in heads:
                bank, f = yield from spare()
                for o, s in ((0, 0), (128, 128), (256, 256)):
                    tt = pe(lambda e, o=o, s=s: e.transpose(bank[:, o:o + 128], Wb[:, s:s + 128], ident), wt, *f)
                banks.append((bank, tt))
            yield
            turned = []
            for (Wb, wt), (bank, tt) in zip(heads, banks):
                WT, w = tmp.get()
                a = act(lambda e: e.activation(WT[:, 0:384], bank[:, 0:384], ACT.Copy), tt, *w)
                misc.put(bank, a)
                tmp.put(Wb, tt)
                turned.append((WT, a))
            yield from pause(2)
            return turned

        def diff_head(h):
            st = SM[:, 16 + 16 * h:32 + 16 * h]
            late = False
            yield from pause(2)
            Ps = []
            for c in range(2):
                bank, f = yield from spare()
                lo_, hi_ = 64 * c, 64 * c + 64
                mm(bank[:, 0:384], Ir, Dr, True, False, dr_tok[0], *f)
                mm(bank[:, 0:128], QA[lo_:hi_, h * T:h * T + 128], KA[lo_:hi_, h * T:h * T + 128], False, False, a_tok)
                tt = mm(bank[:, 128:384], QA[lo_:hi_, h * T + 128:(h + 1) * T], KA[lo_:hi_, h * T:(h + 1) * T],
                        False, True, sig=True)
                yield
                for o, n, i in ((0, 128, 0), (128, 256, 1)):
                    cm = dve(lambda e, o=o, n=n, i=i, bank=bank, c=c: e.tensor_reduce(
                        st[:, 2 * c + i:2 * c + i + 1], bank[:, o:o + n], AX, ALU.max, negate=True), tt)
                cm = dve(lambda e: e.tensor_scalar(st[:, 2 * c:2 * c + 2], st[:, 2 * c:2 * c + 2], slopes[h], None, ALU.mult), cm)
                yield
                Pb, w = tmp.get()
                for o, n, i in ((0, 128, 0), (128, 256, 1)):
                    a = act(lambda e, o=o, n=n, i=i, bank=bank, c=c, Pb=Pb: e.activation(
                        Pb[:, o:o + n], bank[:, o:o + n], ACT.Exp, bias=st[:, 2 * c + i:2 * c + i + 1], scale=slopes[h],
                        accum_out=st[:, 4 + 2 * c + i:5 + 2 * c + i]), cm, *w)
                misc.put(bank, a)
                Ps.append(Pb)
                yield
            r = dve(lambda e: e.reciprocal(st[:, 8:12], st[:, 4:8]), a)
            r0 = dve(lambda e: e.tensor_scalar(st[:, 8:10], st[:, 8:10], inv, None, ALU.mult), r, *lam_ok)
            r1 = dve(lambda e: e.tensor_scalar(st[:, 10:12], st[:, 10:12], nlam, None, ALU.mult), r)
            for o, n, i in ((0, 128, 0), (128, 256, 1)):
                m = dve(lambda e, o=o, n=n, i=i: e.tensor_scalar(Ps[1][:, o:o + n], Ps[1][:, o:o + n],
                                                                 st[:, 10 + i:11 + i], None, ALU.mult), r1)
                wt = dve(lambda e, o=o, n=n, i=i: e.scalar_tensor_tensor(
                    Ps[0][:, o:o + n], Ps[0][:, o:o + n], st[:, 8 + i:9 + i], Ps[1][:, o:o + n], ALU.mult, ALU.add), m, r0)
            tmp.put(Ps[1], wt)
            yield from pause(4)
            WT, a = (yield from turn([(Ps[0], wt)]))[0]
            while not av_tok:
                late = True
                yield
            if late:
                yield from pause(1 + 3 * h)
            bank, f = yield from spare()
            mm(bank[:, 0:T], VA[:, h * P:(h + 1) * P], WT[:, 0:256], True, False, a, av_tok[0], *f)
            tt = mm(bank[:, 128:256], VA[:, 1024 + h * P:1024 + (h + 1) * P], WT[:, 256:384], False, True, sig=True)
            tmp.put(WT, tt)
            pv_tok.append(tt)
            yield from scaled(bank, tt, ones, 1.0 / 128, eps_a, gain_a, h, *lam_ok)

        pv_tok = []
        for h in range(8):
            queue.append(holding(2, diff_head(h), 5))
        av_tok = []
        av_tok.append(values(VA, 8)[0])
        b_tok, t = qk(QB, KB, 4)
        NM, CMk, TRI2, BD, J = k2("nm"), k2("cm"), k2("tri2"), k2("bd"), k2("flip")
        bv_tok, cv_tok = [], []
        def stick_pair(i):
            yield from pause(2)
            heads = []
            for p in range(2):
                lo_, hi_ = 64 * p, 64 * p + 64
                bank, f = yield from spare()
                mm(bank[:, 0:256], KB[lo_:hi_, i * T:i * T + 128], QB[lo_:hi_, i * T:(i + 1) * T], True, True, b_tok, *f)
                tt = mm(bank[:, 256:384], KB[lo_:hi_, i * T + 128:(i + 1) * T], QB[lo_:hi_, i * T + 128:(i + 1) * T],
                        True, True, sig=True)
                heads.append((bank, tt))
            yield
            banks, heads = heads, []
            for bank, tt in banks:
                (z, w), (q, w2) = tmp.get(), tmp.get()
                z_, q_ = z[:, 0:384], q[:, 0:384]
                c = dve(lambda e: e.tensor_tensor(z_, bank[:, 0:384], CMk, ALU.mult), tt, *w)
                misc.put(bank, c)
                c = dve(lambda e: e.scalar_tensor_tensor(q_, z_, -1.0, z_, ALU.mult, ALU.max), c, *w2)
                heads.append((z, q, c))
            yield from pause(2)
            for z, q, c in heads:
                a0 = act(lambda e: e.activation(q[:, 0:384], q[:, 0:384], ACT.Exp, scale=-1.0), c)
            a = []
            for z, q, c in heads:
                a.append(act(lambda e: e.activation(q[:, 0:384], q[:, 0:384], ACT.Ln, bias=1.0), a0))
            yield from pause(4)
            cs = []
            for (z, q, c), a_ in zip(heads, a):
                z_, q_ = z[:, 0:384], q[:, 0:384]
                c = dve(lambda e: e.scalar_tensor_tensor(q_, z_, 0.0, q_, ALU.max, ALU.add), a_)
                cs.append(dve(lambda e: e.tensor_tensor(q_, q_, NM, ALU.mult), c))
            yield from pause(3)
            sums = []
            for (z, q, c), c2_ in zip(heads, cs):
                bank, f = yield from spare()
                mm(bank[:, 0:256], TRI2, q[:, 0:256], True, False, c2_, *f)
                mm(bank[:, 128:256], ones, q[:, 256:384], False, True)
                tt = mm(bank[:, 256:384], TRI2, q[:, 256:384], True, True, sig=True)
                tmp.put(q, tt)
                sums.append((bank, tt))
            yield
            cs = []
            for (z, q, c), (bank, tt) in zip(heads, sums):
                z_ = z[:, 0:384]
                cs.append(dve(lambda e: e.tensor_tensor(z_, bank[:, 0:384], z_, ALU.add), tt))
                misc.put(bank, cs[-1])
            yield from pause(2)
            a = []
            for (z, q, c), c2_ in zip(heads, cs):
                z_ = z[:, 0:384]
                a.append(act(lambda e: e.activation(z_, z_, ACT.Exp), c2_))
            yield from pause(2)
            cs = []
            for (z, q, c), a_ in zip(heads, a):
                z_ = z[:, 0:384]
                cs.append(dve(lambda e: e.tensor_tensor(z_, z_, CMk, ALU.mult), a_))
            yield from pause(2)
            while not bv_tok:
                yield
            o_bank, f = yield from spare()
            for p, (z, q, c) in enumerate(heads):
                h = 2 * i + p
                o = o_bank[64 * p:64 * p + 64, 0:T]
                mm(o, VB[:, h * 64:h * 64 + 64], z[:, 0:256], True, False, cs[p], bv_tok[0], *f)
                tt = mm(o[:, 128:256], VB[:, 512 + h * 64:512 + h * 64 + 64], z[:, 256:384], False, True, sig=True)
                tmp.put(z, tt)
            yield from scaled(o_bank, tt, BD, 1.0 / 64, col("eps6"), col("sb_norm_2", i), 8 + i)

        def band_pair(i):
            yield from pause(2)
            heads = []
            for p in range(2):
                h = 2 * i + p
                lo_, hi_ = 64 * p, 64 * p + 64
                bank, f = yield from spare()
                hk_ = HK[:, h * T:(h + 1) * T]
                mm(bank[:, 0:128], J, hk_[:, 128:256], True, False, (s_h, 16), *f)
                mm(bank[:, 0:128], QC[lo_:hi_, i * T:i * T + 128], KC[lo_:hi_, i * T:i * T + 128], False, False, c_tok)
                mm(bank[:, 64:128], Ir, MCr, False, True, mc_tok[0])
                mm(bank[:, 128:384], J, hk_, True, False)
                mm(bank[:, 128:384], QC[lo_:hi_, i * T + 128:(i + 1) * T], KC[lo_:hi_, i * T:(i + 1) * T], False, False)
                tt = mm(bank[:, 320:384], Ir, MCr, False, True, sig=True)
                heads.append((bank, tt))
            yield
            banks, heads = heads, []
            for p, (bank, tt) in enumerate(banks):
                st = SM[:, 96 + 16 * (2 * i + p):112 + 16 * (2 * i + p)]
                for o, n, k in ((0, 128, 0), (128, 256, 1)):
                    cm = dve(lambda e: e.tensor_reduce(st[:, k:k + 1], bank[:, o:o + n], AX, ALU.max, negate=True), tt)
                heads.append((bank, st, cm))
            yield from pause(2)
            banks, heads = heads, []
            for bank, st, cm in banks:
                Pb, w = tmp.get()
                for o, n, k in ((0, 128, 0), (128, 256, 1)):
                    a = act(lambda e: e.activation(Pb[:, o:o + n], bank[:, o:o + n], ACT.Exp, bias=st[:, k:k + 1],
                                                   accum_out=st[:, 2 + k:3 + k]), cm, *w)
                misc.put(bank, a)
                heads.append((Pb, st, a))
            yield from pause(2)
            wts = []
            for Pb, st, a in heads:
                r = dve(lambda e: e.reciprocal(st[:, 4:6], st[:, 2:4]), a)
                for o, n, k in ((0, 128, 0), (128, 256, 1)):
                    wt = dve(lambda e: e.tensor_scalar(Pb[:, o:o + n], Pb[:, o:o + n], st[:, 4 + k:5 + k], None, ALU.mult), r)
                wts.append(wt)
            yield from pause(3)
            turned = yield from turn([(Pb, wt) for (Pb, st, a), wt in zip(heads, wts)])
            while not cv_tok:
                yield
            o_bank, f = yield from spare()
            for p, (WT, a) in enumerate(turned):
                h = 2 * i + p
                o = o_bank[64 * p:64 * p + 64, 0:T]
                mm(o, VC[:, h * 64:h * 64 + 64], WT[:, 0:256], True, False, a, cv_tok[0], *f)
                tt = mm(o[:, 128:256], VC[:, 512 + h * 64:512 + h * 64 + 64], WT[:, 256:384], False, True, sig=True)
                tmp.put(WT, tt)
            yield from scaled(o_bank, tt, BD, 1.0 / 64, col("eps6"), col("ch_norm_2", i), 12 + i)

        for i in range(4):
            queue.append(holding(4, stick_pair(i), 8))
        bv_tok.append(values(VB, 4)[0])
        while len(pv_tok) < 8:
            step()
        act.dma(HK.rearrange("p (h n) -> p h n", h=8), hank_src, s_h, *pv_tok, (s_g, 32))
        c_tok, t = qk(QC, KC, 4, *pv_tok)
        for i in range(4):
            queue.append(holding(3, band_pair(i), 8))
        c_last, t = values(VC, 4, *pv_tok)
        cv_tok.append(c_last)
        H.free = (t,)
        for j in range(8):
            bank, t = mtiles(Y, 8)
            residual(bank, t, j)
        drain()
        room[0] -= 3
        sx = Sum()
        for j in range(8):
            bank, t = mtiles(Y, 8, 2, 8)
            residual(bank, t, j, sx, H, "ffn_norm_2")
        Y.free = (t,)
        sx = ffn(True, col("eps6"), None, None)
        outs = 0
        nx = Norm(sx, col("eps6"), RN)
        for _ in nx.task():
            pass
        early = {}
        for k in range(0, 16, 4):
            early[k] = pool(lambda e: e.tensor_scalar(xt(k), xt(k), col("final_norm_2", k), None, ALU.mult), nx.s.tok, V_OK)
        for k in range(16):
            if k % 4 == 0:
                p = pool(lambda e: e.tensor_tensor(xt(k), xt(k), RN, ALU.mult), nx.ok, early[k])
            else:
                c = dve(lambda e: e.scalar_tensor_tensor(xt(k), xt(k), col("final_norm_2", k), RN, ALU.mult, ALU.mult), nx.ok)
            if k % 4 == 3:
                sp.dma(out[:, (k - 3) * T:(k + 1) * T], xt(k - 3, 4), s_out, c, p)
                outs += 16
        sp(None, (s_out, outs), (s_g, 32), (s_h, 16), sig=False)
        assert state["blk"] == 16 * len(order), (state, len(order))

        with nc.Block() as blk:
            @blk.sync
            def _(e):
                sp.play(e)

            @blk.scalar
            def _(e):
                act.play(e)

            @blk.vector
            def _(e):
                dve.play(e)

            @blk.gpsimd
            def _(e):
                pool.play(e)

            @blk.tensor
            def _(e):
                pe.play(e)


def tiles(w):
    k, n = w.shape
    return w.reshape(k // P, P, n // P, P).transpose(2, 0, 1, 3).reshape(-1, P, P)


def wide(w):
    k, n = w.shape
    return w.reshape(k // P, P, n // T, 2, P).transpose(2, 0, 3, 1, 4).reshape(-1, P, P)


def units(*blocks):
    b = np.concatenate(blocks)
    return np.ascontiguousarray(b.reshape(-1, 16, P, P).transpose(0, 2, 1, 3)).reshape(-1, P, UNIT)


def pairs(*ws):
    n = ws[0].shape[1]
    return [tiles(w[:, c:c + T]) for c in range(0, n, T) for w in ws]


def ffn_units(gate, up, down):
    out = []
    for a0, a1 in PARTS:
        out += pairs(gate[:, a0 * P:a1 * P], up[:, a0 * P:a1 * P])
        out.append(tiles(down[a0 * P:a1 * P]))
    return units(*out)


def columns(v):
    return np.ascontiguousarray(v.reshape(-1, P).T)


def layout(a):
    f = np.float32
    w = a["w_in"][0]
    z, xs, bc = w[:, 0:2048], w[:, 2048:4096], w[:, 4096:5120]
    dt = np.concatenate([w[:, 5120:5152], np.zeros((2048, 96), f)], axis=1)
    su, sb_, sc = w[:, 5152:7200], w[:, 7200:9248], w[:, 9248:11296]
    d = {}
    d["w_in"] = units(*pairs(su, sc, sb_), tiles(bc), tiles(dt), tiles(xs), tiles(z))
    d["w_out"] = units(tiles(a["w_out"][0][2048:]), tiles(a["w_out"][0][:2048]))
    d["w_k"], d["w_v"], d["w_q"] = units(tiles(a["w_k"][0])), units(wide(a["w_v"][0])), units(tiles(a["w_q"][0]))
    d["w_o"] = units(tiles(a["w_o"][0]))
    d["ffn"] = ffn_units(a["w_gate"][0], a["w_up"][0], a["w_down"][0])
    q = a["w_qkv_2"][0]
    parts, at = [], 0
    for n in (1024, 512, 512):
        parts += [tiles(q[:, at:at + 2 * n]), wide(q[:, at + 2 * n:at + 3 * n])]
        at += 3 * n
    d["w_qkv_2"] = units(*parts)
    d["w_o_2"] = units(tiles(a["w_o_2"][0][:1024]), tiles(a["w_o_2"][0][1024:]))
    d["ffn_2"] = ffn_units(a["w_gate_2"][0], a["w_up_2"][0], a["w_down_2"][0])

    def fm(x):
        return np.ascontiguousarray(x.reshape(T, 16, P).transpose(2, 1, 0)).reshape(P, 16 * T)

    d["x"], d["mem"] = fm(a["x"]), fm(a["mem"])
    vec = np.zeros((P, NVEC), f)
    for name, (o, n) in VOFF.items():
        if name in ("a_log", "d_skip"):
            v = np.broadcast_to(a[name].reshape(1, 32), (P, 32))
        elif name == "dt_bias":
            v = np.concatenate([a[name].reshape(32), np.zeros(96, f)]).reshape(P, 1)
        elif name in ("eps5", "eps6"):
            v = np.full((P, 1), 1e-5 if name == "eps5" else 1e-6, f)
        else:
            v = columns(a[name])
        vec[:, o:o + n] = v
    d["vec"] = vec
    i = np.arange(P)
    le = (i[:, None] <= i[None, :]).astype(f)
    one = np.ones((P, P), f)
    d["c1"] = np.concatenate([np.eye(P, dtype=f), le, one, one, np.where(le > 0, 0, NEG).astype(f)], axis=1)
    lt = (i[:, None] < i[None, :]).astype(f)
    cm = np.concatenate([lt, one, lt], axis=1)
    qi, ki = i[:, None], np.arange(T)[None, :]
    d0 = np.where(ki[:, :P] // 64 <= qi // 64, -np.abs(qi - ki[:, :P]), NEG)
    d1 = np.where(ki // 64 <= (qi + P) // 64, -np.abs(qi + P - ki), NEG)
    mc = np.where(np.broadcast_to(qi < 64, (P, 64)), NEG, 0.0)
    lam = np.concatenate([a[n].reshape(1, 64) for n in ("lambda_q1_2", "lambda_k1_2", "lambda_q2_2", "lambda_k2_2")], axis=1)
    bd = (i[:, None] // 64 == i[None, :] // 64).astype(f)
    d["c2"] = np.concatenate([bd, le.T, np.eye(P, dtype=f)[::-1], -cm, cm, d0, d1, mc, np.broadcast_to(lam, (P, 256))],
                             axis=1).astype(f)
    d["rel"] = np.ascontiguousarray(a["rel_bias_2"][0][:, ::-1])
    return d


def kernel(**inputs):
    import concourse.bacc as _bacc
    from concourse import mybir as _mybir
    from concourse.bass_utils import run_bass_kernel_spmd as _run

    d = layout({k: np.asarray(v) for k, v in inputs.items()})
    nc = _bacc.Bacc("TRN2", target_bir_lowering=False, num_devices=1)
    arrays, aps = {}, {}
    for name, v in d.items():
        arrays[f"in_{name}"] = v
        aps[name] = nc.dram_tensor(f"in_{name}", v.shape, _mybir.dt.float32, kind="ExternalInput").ap()
    out = nc.dram_tensor("out_0", [P, 16 * T], _mybir.dt.float32, kind="ExternalOutput").ap()
    build(nc, aps, out)
    r = _run(nc, [arrays], core_ids=[0])
    y = r.results[0]["out_0"]
    return np.ascontiguousarray(y.reshape(P, 16, T).transpose(2, 1, 0)).reshape(1, T, 16 * P)
```
